# Optimizing a Trainium2 kernel written in Bass

```python
import jax, jax.numpy as jnp
from jax import lax
import numpy as np

D_MODEL = 1024
BATCH = 1
SEQ = 512
DEPTH = 1

CHUNK = 64
GMLP_BLOCK = 128
GMLP_GROUPS = 8
GMLP_WIDTH = D_MODEL
GMLP_GROUP_WIDTH = GMLP_WIDTH // GMLP_GROUPS
HEAD_DIM = 64
N_HEADS = D_MODEL // HEAD_DIM
N_KV_HEADS = 4
WINDOW = 128
WINDOW_CHUNKS = WINDOW // CHUNK
ATTN_WIDTH = N_HEADS * HEAD_DIM
KV_WIDTH = N_KV_HEADS * HEAD_DIM
IN_SPLITS = (GMLP_WIDTH, GMLP_WIDTH, ATTN_WIDTH, KV_WIDTH, KV_WIDTH, D_MODEL, D_MODEL)
IN_WIDTH = sum(IN_SPLITS)
N_GROUPS = 4
EXPERTS_PER_GROUP = 8
N_EXPERTS = N_GROUPS * EXPERTS_PER_GROUP
TOP_K = 2
D_EXPERT = D_MODEL // 2
EPS = 1e-6
NEG_INF = -1e30

kernel_name = "hybrid_gmlp_swa_hmoe_block"

def rmsnorm(x, g):
    xf = x.astype(jnp.float32)
    r = lax.rsqrt(jnp.mean(xf * xf, axis=-1, keepdims=True) + EPS)
    return (xf * r).astype(x.dtype) * g

def layernorm(x, g, b):
    xf = x.astype(jnp.float32)
    mu = jnp.mean(xf, axis=-1, keepdims=True)
    var = jnp.mean(jnp.square(xf - mu), axis=-1, keepdims=True)
    return ((xf - mu) * lax.rsqrt(var + EPS)).astype(x.dtype) * g + b

def alibi_slopes(n_heads):
    return np.power(2.0, -8.0 * (np.arange(n_heads) + 1) / n_heads).astype(np.float32)

def gmlp_spatial_gating(u, v, ln_g, ln_b, w_s, b_s):
    B, S, _ = v.shape
    nb = S // GMLP_BLOCK
    vn = layernorm(v, ln_g, ln_b).reshape(B, nb, GMLP_BLOCK, GMLP_GROUPS, GMLP_GROUP_WIDTH)
    pos_chunk = np.arange(GMLP_BLOCK) // CHUNK
    mask = pos_chunk[None, :] <= pos_chunk[:, None]
    w = jnp.where(mask[None], w_s, jnp.zeros_like(w_s))
    sv = jnp.einsum('gij,bnjgc->bnigc', w, vn) + b_s.T[None, None, :, :, None]
    return u * sv.reshape(B, S, GMLP_WIDTH)

def sliding_window_attention(q, k, v, sinks):
    B, S = q.shape[:2]
    nc = S // CHUNK
    rep = N_HEADS // N_KV_HEADS
    band = WINDOW_CHUNKS * CHUNK
    qb = q.reshape(B, nc, CHUNK, N_KV_HEADS, rep, HEAD_DIM)
    pad = ((0, 0), ((WINDOW_CHUNKS - 1) * CHUNK, 0), (0, 0), (0, 0))
    kc = jnp.pad(k, pad).reshape(B, nc + WINDOW_CHUNKS - 1, CHUNK, N_KV_HEADS, HEAD_DIM)
    vc = jnp.pad(v, pad).reshape(B, nc + WINDOW_CHUNKS - 1, CHUNK, N_KV_HEADS, HEAD_DIM)
    kband = jnp.concatenate([kc[:, w:w + nc] for w in range(WINDOW_CHUNKS)], axis=2)
    vband = jnp.concatenate([vc[:, w:w + nc] for w in range(WINDOW_CHUNKS)], axis=2)
    scores = jnp.einsum('bnqkrd,bnskd->bnkrqs', qb, kband,
                        preferred_element_type=jnp.float32) * (HEAD_DIM ** -0.5)
    qpos = (WINDOW_CHUNKS - 1) * CHUNK + np.arange(CHUNK)
    kpos = np.arange(band)
    dist = np.abs(qpos[:, None] - kpos[None, :]).astype(np.float32)
    alibi = -alibi_slopes(N_HEADS).reshape(N_KV_HEADS, rep, 1, 1) * dist
    valid = (np.arange(nc)[:, None] + kpos[None, :] // CHUNK - (WINDOW_CHUNKS - 1)) >= 0
    scores = jnp.where(valid[None, :, None, None, None, :], scores + alibi, NEG_INF)
    sink = sinks.astype(jnp.float32).reshape(1, 1, N_KV_HEADS, rep, 1, 1)
    m = jnp.maximum(jnp.max(scores, axis=-1, keepdims=True), sink)
    p = jnp.exp(scores - m)
    denom = jnp.sum(p, axis=-1, keepdims=True) + jnp.exp(sink - m)
    probs = (p / denom).astype(v.dtype)
    out = jnp.einsum('bnkrqs,bnskd->bnqkrd', probs, vband)
    return out.reshape(B, S, ATTN_WIDTH)

def hierarchical_moe(x, w_rg, b_rg, w_re, b_re, w_gate, w_up, w_down):
    B, S, D = x.shape
    n = B * S
    xf = x.reshape(n, D)
    glog = (xf @ w_rg + b_rg).astype(jnp.float32)
    gprob = jax.nn.softmax(glog, axis=-1)
    gsel = jnp.argmax(glog, axis=-1)
    pg = jnp.take_along_axis(gprob, gsel[:, None], axis=-1)
    elog_all = (xf @ w_re + b_re).astype(jnp.float32).reshape(n, N_GROUPS, EXPERTS_PER_GROUP)
    elog = jnp.take_along_axis(elog_all, gsel[:, None, None], axis=1)[:, 0]
    topv, topi = lax.top_k(elog, TOP_K)
    tw = jax.nn.softmax(topv, axis=-1) * pg
    eid = gsel[:, None] * EXPERTS_PER_GROUP + topi
    combine = jnp.sum(jax.nn.one_hot(eid, N_EXPERTS, dtype=jnp.float32) * tw[..., None], axis=1)
    combine = combine.astype(x.dtype)
    y = jnp.zeros_like(xf)
    for e in range(N_EXPERTS):
        h = jax.nn.silu(xf @ w_gate[e]) * (xf @ w_up[e])
        y = y + combine[:, e:e + 1] * (h @ w_down[e])
    return y.reshape(B, S, D)

def setup_inputs(seed: int = 0) -> dict:
    key = jax.random.key(seed)
    ks = jax.random.split(key, 24)
    f32 = jnp.float32
    L = DEPTH

    def nrm(k, shape, scale):
        return jax.random.normal(k, shape, f32) * scale

    return {
        "x": nrm(ks[0], (BATCH, SEQ, D_MODEL), 1.0),
        "norm_mix_g": 1.0 + nrm(ks[1], (L, D_MODEL), 0.02),
        "w_in": nrm(ks[2], (L, D_MODEL, IN_WIDTH), D_MODEL ** -0.5),
        "gate_bias": nrm(ks[3], (L, 2 * D_MODEL), 0.1),
        "gmlp_ln_g": 1.0 + nrm(ks[4], (L, GMLP_WIDTH), 0.02),
        "gmlp_ln_b": nrm(ks[5], (L, GMLP_WIDTH), 0.02),
        "gmlp_w_s": nrm(ks[6], (L, GMLP_GROUPS, GMLP_BLOCK, GMLP_BLOCK), 0.5 * GMLP_BLOCK ** -0.5),
        "gmlp_b_s": 1.0 + nrm(ks[7], (L, GMLP_GROUPS, GMLP_BLOCK), 0.1),
        "attn_sinks": nrm(ks[8], (L, N_HEADS), 0.5),
        "w_branch_a": nrm(ks[9], (L, GMLP_WIDTH, D_MODEL), GMLP_WIDTH ** -0.5),
        "w_branch_b": nrm(ks[10], (L, ATTN_WIDTH, D_MODEL), ATTN_WIDTH ** -0.5),
        "w_out": nrm(ks[11], (L, D_MODEL, D_MODEL), D_MODEL ** -0.5),
        "norm_ffn_g": 1.0 + nrm(ks[12], (L, D_MODEL), 0.02),
        "w_router_group": nrm(ks[13], (L, D_MODEL, N_GROUPS), D_MODEL ** -0.5),
        "b_router_group": nrm(ks[14], (L, N_GROUPS), 0.01),
        "w_router_expert": nrm(ks[15], (L, D_MODEL, N_EXPERTS), D_MODEL ** -0.5),
        "b_router_expert": nrm(ks[16], (L, N_EXPERTS), 0.01),
        "w_gate": nrm(ks[17], (L, N_EXPERTS, D_MODEL, D_EXPERT), D_MODEL ** -0.5),
        "w_up": nrm(ks[18], (L, N_EXPERTS, D_MODEL, D_EXPERT), D_MODEL ** -0.5),
        "w_down": nrm(ks[19], (L, N_EXPERTS, D_EXPERT, D_MODEL), D_EXPERT ** -0.5),
        "norm_final_g": 1.0 + nrm(ks[20], (D_MODEL,), 0.02),
    }

def reference(x, norm_mix_g, w_in, gate_bias, gmlp_ln_g, gmlp_ln_b, gmlp_w_s, gmlp_b_s,
              attn_sinks, w_branch_a, w_branch_b, w_out, norm_ffn_g, w_router_group,
              b_router_group, w_router_expert, b_router_expert, w_gate, w_up, w_down,
              norm_final_g):
    B, S, _ = x.shape
    split_idx = [int(i) for i in np.cumsum(IN_SPLITS)[:-1]]
    h = x
    for l in range(DEPTH):
        xn = rmsnorm(h, norm_mix_g[l])
        proj = xn @ w_in[l]
        zu, zv, q, k, va, ga, gb = jnp.split(proj, split_idx, axis=-1)
        u = jax.nn.gelu(zu, approximate=False)
        v = jax.nn.gelu(zv, approximate=False)
        y_a = gmlp_spatial_gating(u, v, gmlp_ln_g[l], gmlp_ln_b[l], gmlp_w_s[l], gmlp_b_s[l]) @ w_branch_a[l]
        att = sliding_window_attention(q.reshape(B, S, N_HEADS, HEAD_DIM),
                                       k.reshape(B, S, N_KV_HEADS, HEAD_DIM),
                                       va.reshape(B, S, N_KV_HEADS, HEAD_DIM),
                                       attn_sinks[l])
        y_b = att @ w_branch_b[l]
        gates = jax.nn.sigmoid(jnp.concatenate([ga, gb], axis=-1) + gate_bias[l])
        g_a, g_b = jnp.split(gates, 2, axis=-1)
        h = h + (g_a * y_a + g_b * y_b) @ w_out[l]
        hn = rmsnorm(h, norm_ffn_g[l])
        h = h + hierarchical_moe(hn, w_router_group[l], b_router_group[l], w_router_expert[l],
                                 b_router_expert[l], w_gate[l], w_up[l], w_down[l])
    return rmsnorm(h, norm_final_g)


_drawn_inputs = setup_inputs


def setup_inputs(seed=0):
    import zlib

    import numpy as np

    out = dict(_drawn_inputs(seed))
    spreads = {}
    factors = {'gmlp_ln_g': 3.913,
     'gmlp_ln_b': 4.912,
     'attn_sinks': 3.509,
     'b_router_group': 4.166,
     'b_router_expert': 3.314,
     'norm_final_g': 2.95}
    for name, (base, spread) in spreads.items():
        noise = np.random.default_rng([zlib.crc32(name.encode()), seed]).standard_normal(out[name].shape)
        drawn = base * np.exp(spread * noise) if base else spread * noise
        out[name] = __import__('jax').numpy.asarray(drawn.astype(out[name].dtype))
    for name, factor in factors.items():
        out[name] = (out[name] * factor).astype(out[name].dtype)
    return out
```

```python
from contextlib import ExitStack

import numpy as np

import concourse.bass as bass
from concourse import mybir

F32 = mybir.dt.float32
F32R = mybir.dt.float32r
BF16 = mybir.dt.bfloat16
I32 = mybir.dt.int32
ALU = mybir.AluOpType
ACT = mybir.ActivationFunctionType
AX = mybir.AxisListType

P = 128
EPS = 1e-6
MASKED = -1e30
KB = 1024


def build_block(nc, x, norm_mix_g, w_in, gate_bias, gmlp_ln_g, gmlp_ln_b, gmlp_w_s, gmlp_b_s,
                attn_sinks, w_branch_a, w_branch_b, w_out, norm_ffn_g, w_router_group,
                b_router_group, w_router_expert, b_router_expert, w_gate, w_up, w_down,
                norm_final_g, out):
    _, SEQ, D = x.shape
    TT = SEQ // P
    KT = D // P
    GROUPS = gmlp_w_s.shape[1]
    H = attn_sinks.shape[1]
    KVW = (w_in.shape[2] - 5 * D) // 2
    HD = D // H
    KVH = KVW // HD
    REP = H // KVH
    BAND = P + HD
    NG = w_router_group.shape[2]
    NE = w_router_expert.shape[2]
    EPG = NE // NG
    DE = w_gate.shape[3]
    FT = DE // P
    ROWS = 64
    PAIRS = NE // 2
    OV_PAIRS = -(-((2 * SEQ - NE) // ROWS) // 2)
    OV_TILES = 2 * OV_PAIRS
    MAX_OV = SEQ // ROWS - 1
    NR = NG + NE
    SCALE = float(HD) ** -0.5
    slopes = [float(np.float32(2.0 ** (-8.0 * (h + 1) / H))) for h in range(H)]
    assert GROUPS == KT == 8 and TT == 4 and KVH == 4 and REP == 4 and HD == ROWS == 64 and FT == 4

    packed_y = nc.dram_tensor("packed_y", [(NE + OV_TILES) * ROWS, D], F32).ap()

    base = -(-nc.sbuf_base // 64) * 64

    def at(name, shape, dt, kb):
        return nc.alloc_sbuf_tensor_at(name, shape, dt, offset=base + int(kb * KB))

    xnT_hi = at("xnT_hi", [P, KT, SEQ], F32R, 0)
    xnT_lo = at("xnT_lo", [P, KT, SEQ], F32R, 16)
    v_tok = at("v_tok", [P, TT, D], F32, 32)
    xg = at("xg", [P, KT, SEQ], F32, 32)
    attT_hi = at("attT_hi", [P, KT, SEQ], F32R, 32)
    attT_lo = at("attT_lo", [P, KT, SEQ], F32R, 48)
    dist_i = at("dist_i", [P, BAND], I32, 48)
    dist = at("dist", [P, BAND], F32, 49)
    band_mask = at("band_mask", [P, BAND], F32, 50)
    gated = at("gated", [P, SEQ], F32, 52)
    ws_nat = at("ws_nat", [P, GROUPS, P], F32, 64)
    qT = at("qT", [P, KT, SEQ], F32, 64)
    ln_g = at("ln_g", [P, D], F32, 80)
    ln_b = at("ln_b", [P, D], F32, 84)
    vaT = at("vaT", [P, 2, SEQ], F32, 88)
    bs_row = at("bs_row", [1, GROUPS, P], F32, 92)
    branch_a = at("branch_a", [P, KT, SEQ], F32, 80)
    x_tok = at("x_tok", [P, TT, D], F32, 96)
    xn_tok = at("xn_tok", [P, TT, D], F32, 112)
    spT_hi = at("spT_hi", [P, KT, SEQ], F32R, 96)
    spT_lo = at("spT_lo", [P, KT, SEQ], F32R, 112)
    mgT_hi = at("mgT_hi", [P, KT, SEQ], F32R, 96)
    mgT_lo = at("mgT_lo", [P, KT, SEQ], F32R, 112)
    raw = [at(f"raw{b}", [P, 2048], F32, 128 + 8 * b) for b in range(2)]
    whi = [at(f"whi{b}", [P, 2048], F32R, 144 + 8 * b) for b in range(2)]
    wlo = [at(f"wlo{b}", [P, 2048], F32R, 160 + 8 * b) for b in range(2)]
    kT = at("kT", [P, 2, SEQ], F32, 176)
    va_tok = at("va_tok", [P, TT, KVW], F32, 180)
    probs = [at(f"probs{b}", [P, REP, 2 * P], F32, 184 + 4 * b) for b in range(2)]
    probsT = [at(f"probsT{b}", [P, 768], F32, 192 + 3 * b) for b in range(2)]
    merged = at("merged", [P, SEQ], F32, 192)
    wsT = at("wsT", [P, GROUPS, P], F32, 198)
    alibi = at("alibi", [P, H, BAND], F32, 202)
    gbuf = [at(f"gbuf{b}", [P, SEQ], F32, 214 + 2 * b) for b in range(2)]
    vec_rows = at("vec_rows", [3 * KT, P], F32, 214)
    ident = at("ident", [P, P], F32, 218)
    small = at("small", [P, 200], F32, 218.5)
    ones_row = at("ones_row", [1, P], F32, 219.3125)
    W = [at(f"W{u}", [P, 8 * DE], F32, 16 * u) for u in range(6)]
    hn_part = [at(f"hn_part{j}", [P, TT, KT, P], BF16, 96 + 8 * j) for j in range(3)]
    packT = at("packT", [P, KT, P], F32, 120)
    y_rows = at("y_rows", [P, D], F32, 124)
    hn = at("hn", [P, TT, KT, P], F32, 128)
    hnT = at("hnT", [P, KT, SEQ], F32, 144)
    hn_rest = at("hn_rest", [P, TT, KT, P], F32, 160)
    h_tok = at("h_tok", [P, TT, D], F32, 176)
    ffn_g = at("ffn_g", [P, D], F32, 192)
    w_router = at("w_router", [P, KT, NR], F32, 196)
    b_router = at("b_router", [NR, 1], F32, 197.5)
    logitsT = at("logitsT", [NR, SEQ], F32, 214)
    squares = at("squares", [P, D], F32, 214)
    logits = at("logits", [P, TT, NR], F32, 198)
    silu_g = at("silu_g", [P, DE], F32, 200)
    act_rows = at("act_rows", [P, FT, P], F32, 202)
    actT = at("actT", [P, FT, P], F32, 204)
    onehot = at("onehot", [P, TT, P], BF16, 206)
    onehot_half = at("onehot_half", [P, TT, P], F32, 128)
    row_iota = at("row_iota", [P, P], F32, 207.5)
    final_g = at("final_g", [P, D], F32, 144)
    y_first = at("y_first", [P, TT, D], F32, 0)
    y_second = at("y_second", [P, TT, D], F32, 16)
    result = at("result", [P, TT, D], F32, 32)

    taken = [0]

    def col(n):
        taken[0] += n
        assert taken[0] <= 200
        return small[:, taken[0] - n:taken[0]]

    mix_g, gate_b, sinks = col(KT), col(2 * KT), col(H)
    mean_sq, rstd, root_work = col(TT), col(TT), col(TT)
    ln_stats, ln_mv = col(TT * 12), col(TT * 2)
    neg_max, sink_e, denom = ([col(REP) for _ in range(2)] for _ in range(3))
    w_first, w_second, row_first, row_second = col(TT), col(TT), col(TT), col(TT)

    room = [208.0]

    def temp(name, shape, dt=F32):
        n = int(np.prod(shape[1:])) * 4 / KB
        room[0] += n
        assert room[0] <= 214
        return at(name, shape, dt, room[0] - n)

    em, sel_a, sel_b, cand, rank = (temp(f"route{i}", [P, TT, NE]) for i in range(5))
    picked = temp("picked", [P, TT, NE], BF16)
    expert_iota = temp("expert_iota", [P, NE])
    first_row = temp("first_row", [P, NE])
    counts, tiles_ov, scan_a, scan_b, delta = (temp(f"route_e{i}", [P, NE]) for i in range(5))
    route_t = temp("route_t", [P, 8 * TT])
    r4 = [route_t[:, i * TT:(i + 1) * TT] for i in range(8)]
    gsel, gcand = temp("gsel", [P, TT, NG]), temp("gcand", [P, TT, NG])
    earlier = at("earlier", [P, P], BF16, 199)
    all_ones = at("all_ones", [P, P], BF16, 199.25)
    ov_iota = at("ov_iota", [1, OV_TILES], F32, 199.5)
    ov_cmp = at("ov_cmp", [1, OV_TILES, NE], F32, 202)
    ov_id = at("ov_id", [1, OV_TILES], F32, 199.5625)
    ov_expert = at("ov_expert", [1, OV_TILES], I32, 199.625)
    ov_count = at("ov_count", [1, 1], I32, 199.6875)
    rows_i = at("rows_i", [P, 2 * TT], I32, 199.75)

    ctx = ExitStack()
    with ctx:
        bank = [ctx.enter_context(nc.psum_tensor(f"bank{i}", [P, 512], F32)) for i in range(8)]

        def sem(name):
            return ctx.enter_context(nc.semaphore(name))

        WIDE, TALL = 4, 8
        units = []

        def raw_view(c, kt):
            return raw[c % 2][:, :].rearrange("p (k n) -> p k n", k=kt)

        def add_unit(kt, moves):
            c = len(units)
            units.append([(dst(raw_view(c, kt)), src) for dst, src in moves])

        whole = lambda v: v
        for n in range(2):
            for kh in range(2):
                add_unit(WIDE, [(whole, w_in[0, kh * 512:(kh + 1) * 512, D + n * 512:D + (n + 1) * 512]
                                 .rearrange("(k p) n -> p k n", p=P))])
        for u in range(4):
            moves = []
            for m in range(2):
                for s in range(2):
                    head = 8 * (u // 2) + 4 * s + 2 * (u % 2) + m
                    moves.append((lambda v, m=m, s=s: v[:, :, m * P + s * HD:m * P + (s + 1) * HD],
                                  w_in[0, :, 2 * D + head * HD:2 * D + (head + 1) * HD]
                                  .rearrange("(k p) n -> p k n", p=P)))
            add_unit(TALL, moves)

        def tall(w, c0):
            add_unit(TALL, [(whole, w[:, c0:c0 + 256].rearrange("(k p) n -> p k n", p=P))])

        tall(w_in[0], 3 * D)
        tall(w_in[0], 3 * D + KVW)
        for u in range(4):
            tall(w_in[0], u * 256)
        for u in range(4):
            tall(w_in[0], 3 * D + 2 * KVW + u * 256)
            tall(w_branch_a[0], u * 256)
        for u in range(4):
            tall(w_in[0], 4 * D + 2 * KVW + u * 256)
            by_head = w_branch_b[0].rearrange("(p s r q) n -> s q p r n", p=2, s=2, r=REP, q=HD)
            moves = []
            for s in range(2):
                for pp in range(2):
                    moves.append((lambda v, s=s, pp=pp: v[s * HD:(s + 1) * HD, pp * REP:(pp + 1) * REP, :],
                                  by_head[s, :, pp, :, u * 256:(u + 1) * 256]))
            add_unit(TALL, moves)
        for n in range(2):
            for kh in range(2):
                add_unit(WIDE, [(whole, w_out[0, kh * 512:(kh + 1) * 512, n * 512:(n + 1) * 512]
                                 .rearrange("(k p) n -> p k n", p=P))])
        ZV, Q, KVA, ZU, GA, GB, WO = 0, 4, 8, 10, 14, 22, 30
        UNITS = len(units)
        landed = []
        for c in range(UNITS):
            landed.append((landed[c - 2] if c >= 2 else 0) + 16 * len(units[c]))

        x_loaded, x_reloaded = sem("x_loaded"), sem("x_reloaded")
        consts_loaded, late_loaded = sem("consts_loaded"), sem("late_loaded")
        unit_loaded = [sem("unit_loaded0"), sem("unit_loaded1")]
        hi_split, lo_split = sem("hi_split"), sem("lo_split")
        half_used = sem("half_used")
        ident_made, iota_made, route_iotas_made = sem("ident_made"), sem("iota_made"), sem("route_iotas_made")
        vecs_psum = sem("vecs_psum")
        square_summed, normed = sem("square_summed"), sem("normed")
        xnT_psum, xg_ready, xhi_ready, xnT_ready = (sem(n) for n in ("xnT_psum", "xg_ready", "xhi_ready", "xnT_ready"))
        act_tile_done, act_tile_read = sem("act_tile_done"), sem("act_tile_read")
        dve_tile_done, gate_used = sem("dve_tile_done"), sem("gate_used")
        wsT_psum, wsT_ready, ln_ready = sem("wsT_psum"), sem("wsT_ready"), sem("ln_ready")
        va_psum, va_ready = sem("va_psum"), sem("va_ready")
        sv_done, sp_ready = sem("sv_done"), sem("sp_ready")
        alibi_ready, scores_done, scores_read, negmax_ready = (
            sem(n) for n in ("alibi_ready", "scores_done", "scores_read", "negmax_ready"))
        exp_done, probs_ready, turned, probsT_ready = (
            sem(n) for n in ("exp_done", "probs_ready", "turned", "probsT_ready"))
        pv_done, att_ready, merged_ready, h_ready = (
            sem(n) for n in ("pv_done", "att_ready", "merged_ready", "h_ready"))
        dve_step = sem("dve_step")
        hsq_summed, hn_ready, hnT_psum, hnT_a, hnT_b = (
            sem(n) for n in ("hsq_summed", "hn_ready", "hnT_psum", "hnT_a", "hnT_b"))
        part0_ready, rest_ready, part1_ready, part2_ready = (
            sem(n) for n in ("part0_ready", "rest_ready", "part1_ready", "part2_ready"))
        logitsT_done, logitsT_ready, logits_turned = (
            sem(n) for n in ("logitsT_done", "logitsT_ready", "logits_turned"))
        route_sub, route_exp, picked_ready, ranks_done, routed = (
            sem(n) for n in ("route_sub", "route_exp", "picked_ready", "ranks_done", "routed"))
        w_loaded = [sem(f"w_loaded{u}") for u in range(6)]
        half_onehot, onehot_ready = sem("half_onehot"), sem("onehot_ready")
        pack_done, pack_a, pack_b = sem("pack_done"), sem("pack_a"), sem("pack_b")
        gate_done, up_done, silu_ready, rows_ready, rows_turned, actT_ready = (
            sem(n) for n in ("gate_done", "up_done", "silu_ready", "rows_ready", "rows_turned", "actT_ready"))
        y_left, y_right, y_left_ready, y_right_ready, y_stored = (
            sem(n) for n in ("y_left", "y_right", "y_left_ready", "y_right_ready", "y_stored"))
        y_gathered = [sem(f"y_gathered{t}") for t in range(TT)]
        ysq_summed, result_ready, out_stored = sem("ysq_summed"), sem("result_ready"), sem("out_stored")
        dve_final = sem("dve_final")

        def wait_unit_used(eng, c):
            if c < Q:
                if c % 2 == 0:
                    eng.wait_ge(half_used, c // 2 + 1)
                else:
                    eng.wait_ge(act_tile_done, 4 * (c // 2 + 1))
            elif c < GA:
                eng.wait_ge(act_tile_done, 8 + 2 * (c - Q + 1))
            elif c < WO:
                if (c - GA) % 2 == 0:
                    eng.wait_ge(act_tile_done, 28 + (c - GA) + 2)
                else:
                    eng.wait_ge(dve_tile_done, (c - GA) + 1)
            elif c % 2 == 0:
                eng.wait_ge(half_used, 3 + (c - WO) // 2)
            else:
                eng.wait_ge(dve_tile_done, 16 + 4 * ((c - WO) // 2 + 1))

        STEPS = KVH * TT

        def step_of(n):
            return n // (2 * TT), (n // 2) % TT, n % 2

        block = ctx.enter_context(nc.Block())

        @block.sync
        def _(sp):
            sp.dma_start(x_tok[:, :, :], x[0].rearrange("(t p) d -> p t d", p=P)).then_inc(x_loaded, 16)

            def load_unit(c):
                if c >= 2:
                    sp.wait_ge(hi_split, c - 1)
                    sp.wait_ge(lo_split, c - 1)
                for dst, src in units[c]:
                    sp.dma_start(dst, src).then_inc(unit_loaded[c % 2], 16)

            def load_experts(u, w, e0, e1):
                rows = w.shape[2] * w.shape[1] // (8 * DE)
                for s, e in enumerate((e0, e1)):
                    sp.dma_start(W[u + s][:, :].rearrange("p (a n) -> p a n", a=1),
                                 w[0, bass.ds(e, 1), :, :].rearrange("a (p c) n -> p a (c n)", p=P)
                                 ).then_inc(w_loaded[u + s], 16)

            for c in range(UNITS - 2):
                load_unit(c)
            wait_unit_used(sp, WO - 2)
            load_experts(0, w_gate, 0, 1)
            load_unit(UNITS - 2)
            wait_unit_used(sp, WO - 1)
            sp.wait_ge(merged_ready, KT)
            load_experts(2, w_up, 0, 1)
            load_unit(UNITS - 1)
            load_experts(4, w_down, 0, 1)
            with sp.Fori(1, PAIRS) as i:
                sp.wait_ge(gate_done, i)
                load_experts(0, w_gate, 2 * i, 2 * i + 1)
                sp.wait_ge(up_done, i)
                load_experts(2, w_up, 2 * i, 2 * i + 1)
                sp.wait_ge(y_right, i)
                load_experts(4, w_down, 2 * i, 2 * i + 1)
            sp.wait_ge(routed, 1)
            n_over = sp.value_load(ov_count[0:1, 0:1], min_val=0, max_val=OV_TILES)
            with sp.If(n_over > 0):
                with sp.Fori(0, OV_PAIRS) as j:
                    e0 = sp.value_load(ov_expert[0:1, bass.ds(2 * j, 1)], min_val=0, max_val=NE - 1)
                    e1 = sp.value_load(ov_expert[0:1, bass.ds(2 * j + 1, 1)], min_val=0, max_val=NE - 1)
                    sp.wait_ge(gate_done, j + PAIRS)
                    load_experts(0, w_gate, e0, e1)
                    sp.wait_ge(up_done, j + PAIRS)
                    load_experts(2, w_up, e0, e1)
                    sp.wait_ge(y_right, j + PAIRS)
                    load_experts(4, w_down, e0, e1)
            for t in range(TT):
                sp.wait_ge(result_ready, t + 1)
                sp.dma_start(out[0, t * P:(t + 1) * P, :], result[:, t, :]).then_inc(out_stored, 16)
            sp.wait_ge(out_stored, 16 * TT)

        @block.gpsimd
        def _(pool):
            pool.memset(ident[:, :], 0.0).then_inc(ident_made, 1)
            pool.wait_ge(ident_made, 1)
            pool.affine_select(out=ident[:, :], in_=ident[:, :], compare_op=ALU.not_equal, fill=1.0, base=0,
                               pattern=[[-1, P]], channel_multiplier=1).then_inc(ident_made, 1)
            pool.iota(dist_i[:, :], pattern=[[-1, BAND]], base=HD, channel_multiplier=1).then_inc(iota_made, 1)
            pool.wait_ge(att_ready, STEPS // 2)
            pool.wait_ge(h_ready, 1)
            pool.iota(row_iota[:, :], pattern=[[1, P]], base=0, channel_multiplier=0,
                      allow_small_or_imprecise_dtypes=True).then_inc(route_iotas_made, 1)
            pool.iota(expert_iota[:, :], pattern=[[1, NE]], base=0, channel_multiplier=0,
                      allow_small_or_imprecise_dtypes=True).then_inc(route_iotas_made, 1)
            pool.iota(first_row[:, :], pattern=[[ROWS, NE]], base=0, channel_multiplier=0,
                      allow_small_or_imprecise_dtypes=True).then_inc(route_iotas_made, 1)
            pool.iota(ov_iota[:, :], pattern=[[1, OV_TILES]], base=0, channel_multiplier=0,
                      allow_small_or_imprecise_dtypes=True).then_inc(route_iotas_made, 1)
            pool.memset(all_ones[:, :], 1.0).then_inc(route_iotas_made, 1)
            pool.wait_ge(route_iotas_made, 5)
            pool.affine_select(out=earlier[:, :], in_=all_ones[:, :], compare_op=ALU.is_gt, fill=0.0, base=0,
                               pattern=[[1, P]], channel_multiplier=-1).then_inc(route_iotas_made, 1)
            pool.wait_ge(routed, 1)
            n_over = pool.value_load(ov_count[0:1, 0:1], min_val=0, max_val=OV_TILES)

            def gather_y(tiles):
                pool.wait_ge(y_stored, 16 * tiles // 2)
                for t in range(TT):
                    for j, rows in enumerate((y_first, y_second)):
                        pool.indirect_dma_start(
                            out=rows[:, t, :], out_offset=None, in_=packed_y[0:tiles * ROWS, :],
                            in_offset=bass.IndirectOffsetOnAxis(ap=rows_i[:, j * TT + t:j * TT + t + 1], axis=0),
                            bounds_check=tiles * ROWS - 1).then_inc(y_gathered[t], 16)

            with pool.If(n_over > 0):
                gather_y(NE + OV_TILES)
            with pool.If(n_over < 1):
                gather_y(NE)

        @block.tensor
        def _(pe):
            pe.wait_ge(ident_made, 2)
            pe.wait_ge(consts_loaded, 16 * 7)
            pe.transpose(bank[7][:, 0:3 * KT], vec_rows[:, :], ident[0:3 * KT, 0:3 * KT]).then_inc(vecs_psum, 1)
            pe.wait_ge(normed, TT)
            for k in range(KT):
                if k >= 4:
                    pe.wait_ge(xg_ready, k - 3)
                for t in range(TT):
                    mm = pe.transpose(bank[k % 4][:, t * P:(t + 1) * P], xn_tok[:, t, k * P:(k + 1) * P], ident[:, :])
                mm.then_inc(xnT_psum, 1)

            def three(dst, hi_w, lo_w, hi_x, lo_x, start, stop):
                pe.matmul(dst, hi_w, hi_x, start=start, stop=False)
                pe.matmul(dst, hi_w, lo_x, start=False, stop=False)
                return pe.matmul(dst, lo_w, hi_x, start=False, stop=stop)

            def wide_unit(c, kh, xT_hi, xT_lo, done):
                pe.wait_ge(lo_split, c + 1)
                w_h = whi[c % 2][:, :].rearrange("p (k n) -> p k n", k=WIDE)
                w_l = wlo[c % 2][:, :].rearrange("p (k n) -> p k n", k=WIDE)
                for t in range(TT):
                    if c == 0 and t == 0:
                        pe.wait_ge(xnT_ready, KT)
                    if c < Q and kh == 0 and c >= 2:
                        pe.wait_ge(act_tile_read, 2 * c - 3 + t)
                    if c >= WO and kh == 0 and c >= WO + 2:
                        pe.wait_ge(h_ready, 2 * (c - WO) - 3 + t)
                    for k in range(WIDE):
                        kk = kh * WIDE + k
                        ts = slice(t * P, (t + 1) * P)
                        dst = bank[t][:, :]
                        first, last = (kh == 0 and k == 0), (kh == 1 and k == WIDE - 1)
                        pe.matmul(dst, xT_hi[:, kk, ts], w_h[:, k, :], start=first, stop=False)
                        pe.matmul(dst, xT_hi[:, kk, ts], w_l[:, k, :], start=False, stop=False)
                        mm = pe.matmul(dst, xT_lo[:, kk, ts], w_h[:, k, :], start=False, stop=last)
                    if kh == 1:
                        mm.then_inc(done, 1)
                if kh == 0:
                    mm.then_inc(half_used, 1)

            def tall_tile(c, m, dst, xT_hi, xT_lo, done):
                if m == 0:
                    pe.wait_ge(lo_split, c + 1)
                w_h = whi[c % 2][:, :].rearrange("p (k n) -> p k n", k=TALL)
                w_l = wlo[c % 2][:, :].rearrange("p (k n) -> p k n", k=TALL)
                ms = slice(m * P, (m + 1) * P)
                for k in range(KT):
                    mm = three(dst, w_h[:, k, ms], w_l[:, k, ms], xT_hi[:, k, :], xT_lo[:, k, :],
                               k == 0, k == KT - 1)
                mm.then_inc(done, 1)

            def act_tile(c, m, a):
                pe.wait_ge(act_tile_read, a - 1)
                tall_tile(c, m, bank[a % 2][:, :], xnT_hi, xnT_lo, act_tile_done)

            def attention_slot(s):
                if s < STEPS:
                    pair, b, side = step_of(s)
                    if s == 0:
                        pe.wait_ge(act_tile_read, 20)
                    pe.wait_ge(scores_read, s)
                    ps = slice(side * HD, (side + 1) * HD)
                    lo = 0 if b else HD
                    for r in range(REP):
                        mm = pe.matmul(bank[3 + r // 2][:, (r % 2) * BAND + lo:(r % 2 + 1) * BAND],
                                       qT[ps, pair * REP + r, b * P:(b + 1) * P],
                                       kT[ps, pair, b * P - HD + lo:(b + 1) * P], start=True, stop=True)
                    mm.then_inc(scores_done, 1)
                if s >= 4 and s % 2 == 0:
                    n = s - 3
                    pair, b, _ = step_of(n)
                    pe.wait_ge(probsT_ready, n + 1)
                    pe.wait_ge(va_ready, 1)
                    pe.wait_ge(att_ready, n // 2)
                    for own in (True, False) if b else (True,):
                        for side in range(2):
                            kv = 2 * pair + side
                            dst = bank[7][side * HD:(side + 1) * HD, :]
                            if own:
                                mm = pe.matmul(dst, va_tok[:, b, kv * HD:(kv + 1) * HD],
                                               probsT[side][:, 0:REP * P], start=True, stop=(b == 0))
                            else:
                                mm = pe.matmul(dst.rearrange("p (r q) -> p r q", q=P)[:, :, 0:HD],
                                               va_tok[:, b - 1, kv * HD:(kv + 1) * HD],
                                               probsT[side][:, REP * P:].rearrange("p (r q) -> p r q", q=HD),
                                               start=False, stop=True)
                    mm.then_inc(pv_done, 1)
                if 2 <= s < STEPS + 2:
                    n = s - 2
                    _, b, _ = step_of(n)
                    pe.wait_ge(probs_ready, n + 1)
                    pe.wait_ge(probsT_ready, n)
                    for r in range(REP):
                        mm = pe.transpose(bank[5][:, r * P:(r + 1) * P], probs[n % 2][:, r, P:2 * P], ident[:, :])
                    for r in range(REP if b else 0):
                        mm = pe.transpose(bank[6][:, r * HD:(r + 1) * HD], probs[n % 2][0:HD, r, 0:P],
                                          ident[0:HD, 0:HD])
                    mm.then_inc(turned, 1)

            for c in range(ZV, Q):
                wide_unit(c, c % 2, xnT_hi, xnT_lo, act_tile_done)
                if c == 1:
                    pe.wait_ge(consts_loaded, 16 * 7)
                    for g in range(GROUPS):
                        mm = pe.transpose(bank[6 + g // 4][:, (g % 4) * P:(g % 4 + 1) * P], ws_nat[:, g, :], ident[:, :])
                    mm.then_inc(wsT_psum, 1)
            for c in range(Q, ZU):
                for m in range(2):
                    act_tile(c, m, 8 + 2 * (c - Q) + m)
            for c in range(ZU, GA):
                for m in range(2):
                    g = 2 * (c - ZU) + m
                    act_tile(c, m, 20 + g)
                    if g == 0:
                        pe.wait_ge(wsT_ready, 1)
                        pe.wait_ge(act_tile_read, 20)
                        for j in range(2):
                            for t in range(TT):
                                mm = pe.transpose(bank[6 + j][:, t * P:(t + 1) * P], vaT[:, j, t * P:(t + 1) * P], ident[:, :])
                        mm.then_inc(va_psum, 1)
                    pe.wait_ge(ln_ready, TT)
                    pe.wait_ge(gate_used, g)
                    pe.matmul(bank[2][:, :], ones_row[:, :], bs_row[0:1, g:g + 1, :].to_broadcast([1, TT, P]),
                              start=True, stop=False)
                    for b in range(TT):
                        mm = pe.matmul(bank[2][:, b * P:(b + 1) * P], v_tok[:, b, g * P:(g + 1) * P], wsT[:, g, :],
                                       start=False, stop=(b == TT - 1))
                    mm.then_inc(sv_done, 1)
                    if g >= 5:
                        attention_slot(g - 5)
            for u in range(4):
                for m in range(2):
                    act_tile(GA + 2 * u, m, 28 + 2 * u + m)
                    attention_slot(3 + 4 * u + m)
                for m in range(2):
                    if u == 0 and m == 0:
                        pe.wait_ge(sp_ready, KT)
                    d = 2 * u + m
                    pe.wait_ge(gate_used, 8 + d)
                    tall_tile(GA + 2 * u + 1, m, bank[2][:, :], spT_hi, spT_lo, dve_tile_done)
                    attention_slot(5 + 4 * u + m)
            for u in range(4):
                for m in range(2):
                    act_tile(GB + 2 * u, m, 36 + 2 * u + m)
                for m in range(2):
                    if u == 0 and m == 0:
                        pe.wait_ge(att_ready, STEPS // 2)
                    d = 8 + 2 * u + m
                    pe.wait_ge(gate_used, 8 + d - 1)
                    tall_tile(GB + 2 * u + 1, m, bank[2 + d % 2][:, :], attT_hi, attT_lo, dve_tile_done)
            pe.wait_ge(act_tile_read, 44)
            pe.wait_ge(merged_ready, KT)
            for c in range(WO, UNITS):
                wide_unit(c, c % 2, mgT_hi, mgT_lo, dve_tile_done)

            for t in range(TT):
                pe.wait_ge(hn_ready, t + 1)
                if t >= 2:
                    pe.wait_ge(hnT_a, t - 1)
                    pe.wait_ge(hnT_b, t - 1)
                for c in range(KT):
                    mm = pe.transpose(bank[4 + 2 * (t % 2) + c // 4][:, (c % 4) * P:(c % 4 + 1) * P],
                                      hn[:, t, c, :], ident[:, :])
                mm.then_inc(hnT_psum, 1)
            pe.wait_ge(hnT_a, TT)
            pe.wait_ge(hnT_b, TT)
            pe.wait_ge(h_ready, 8)
            pe.wait_ge(late_loaded, 16 * 5)
            for c in range(KT):
                mm = pe.matmul(bank[0][0:NR, :], w_router[:, c, :], hnT[:, c, :], start=(c == 0), stop=(c == KT - 1))
            mm.then_inc(logitsT_done, 1)
            pe.wait_ge(logitsT_ready, 1)
            for t in range(TT):
                mm = pe.transpose(bank[1][:, t * NR:(t + 1) * NR], logitsT[:, t * P:(t + 1) * P], ident[0:NR, 0:NR])
            mm.then_inc(logits_turned, 1)
            pe.wait_ge(picked_ready, 1)
            pe.wait_ge(route_iotas_made, 6)
            for t in range(TT):
                for tp in range(t + 1):
                    mm = pe.matmul(bank[2][:, t * NE:(t + 1) * NE], earlier[:, :] if tp == t else all_ones[:, :],
                                   picked[:, tp, :], start=(tp == 0), stop=(tp == t))
            for t in range(TT):
                mm = pe.matmul(bank[3][:, 0:NE], all_ones[:, :], picked[:, t, :], start=(t == 0), stop=(t == TT - 1))
            mm.then_inc(ranks_done, 1)

            def gather_rows(i):
                pe.wait_ge(onehot_ready, i + 1)
                for c in range(KT):
                    for t in range(TT):
                        for j in range(3):
                            mm = pe.matmul(bank[2 + c // 4][:, (c % 4) * P:(c % 4 + 1) * P],
                                           hn_part[j][:, t, c, :], onehot[:, t, :],
                                           start=(t == 0 and j == 0), stop=(t == TT - 1 and j == 2))
                mm.then_inc(pack_done, 1)

            def project(i, u, dst, done):
                for s in range(2):
                    pe.wait_ge(w_loaded[u + s], 16 * i + 16)
                for c in range(KT):
                    for s in range(2):
                        mm = pe.matmul(dst[s * ROWS:(s + 1) * ROWS, :], packT[:, c, s * ROWS:(s + 1) * ROWS],
                                       W[u + s][:, c * DE:(c + 1) * DE], start=(c == 0), stop=(c == KT - 1))
                mm.then_inc(done, 1)

            def expert_pair(i):
                pe.wait_ge(pack_a, i + 1)
                pe.wait_ge(pack_b, i + 1)
                project(i, 0, bank[0], gate_done)
                project(i, 2, bank[1], up_done)
                gather_rows(i + 1)
                pe.wait_ge(rows_ready, i + 1)
                for c in range(FT):
                    mm = pe.transpose(bank[4][:, c * P:(c + 1) * P], act_rows[:, c, :], ident[:, :])
                mm.then_inc(rows_turned, 1)
                pe.wait_ge(actT_ready, i + 1)
                for s in range(2):
                    pe.wait_ge(w_loaded[4 + s], 16 * i + 16)
                for n, done in enumerate((y_left, y_right)):
                    for c in range(FT):
                        for s in range(2):
                            mm = pe.matmul(bank[5 + n][s * ROWS:(s + 1) * ROWS, :], actT[:, c, s * ROWS:(s + 1) * ROWS],
                                           W[4 + s][:, c * D + n * 512:c * D + (n + 1) * 512],
                                           start=(c == 0), stop=(c == FT - 1))
                    mm.then_inc(done, 1)

            pe.wait_ge(part2_ready, TT)
            gather_rows(0)
            with pe.Fori(0, PAIRS) as i:
                expert_pair(i)
            n_over = pe.value_load(ov_count[0:1, 0:1], min_val=0, max_val=OV_TILES)
            with pe.If(n_over > 0):
                with pe.Fori(PAIRS, PAIRS + OV_PAIRS) as i:
                    expert_pair(i)

        @block.scalar
        def _(act):
            consts = [(vec_rows[0:KT, :], norm_mix_g[0].rearrange("(k p) -> k p", p=P)),
                      (vec_rows[KT:3 * KT, :], gate_bias[0].rearrange("(k p) -> k p", p=P)),
                      (sinks, attn_sinks[0].partition_broadcast(P)),
                      (ws_nat[:, :, :], gmlp_w_s[0].rearrange("g i j -> i g j")),
                      (ln_g[:, :], gmlp_ln_g[0].partition_broadcast(P)),
                      (ln_b[:, :], gmlp_ln_b[0].partition_broadcast(P)),
                      (bs_row[:, :, :], gmlp_b_s)]
            for dst, src in consts:
                act.dma_start(dst, src).then_inc(consts_loaded, 16)
            act.wait_ge(x_loaded, 16)
            for t in range(TT):
                act.activation(xn_tok[:, t, :], x_tok[:, t, :], ACT.Square, scale=float(D) ** -0.5,
                               accum_out=mean_sq[:, t:t + 1]).then_inc(square_summed, 1)
            for k in range(KT):
                act.wait_ge(xg_ready, k + 1)
                act.activation(xnT_hi[:, k, :], xg[:, k, :], ACT.Copy).then_inc(xhi_ready, 1)

            def split_hi(c):
                act.wait_ge(unit_loaded[c % 2], landed[c])
                if c >= 2:
                    wait_unit_used(act, c - 2)
                act.activation(whi[c % 2][:, :], raw[c % 2][:, :], ACT.Copy).then_inc(hi_split, 1)

            def start_unit(c):
                if c + 1 < UNITS:
                    split_hi(c + 1)

            def gate_tile(a, func, **kw):
                act.wait_ge(act_tile_done, a + 1)
                if a - 20 >= 2:
                    act.wait_ge(gate_used, a - 20 - 1)
                act.activation(gbuf[a % 2][:, :], bank[a % 2][:, :], func, **kw).then_inc(act_tile_read, 1)

            def attention_slot(s):
                if 2 <= s < STEPS + 2:
                    n = s - 2
                    _, b, _ = step_of(n)
                    act.wait_ge(turned, n + 1)
                    if n >= 2:
                        act.wait_ge(pv_done, n // 2)
                    last = act.activation(probsT[n % 2][:, 0:512], bank[5][:, :], ACT.Copy)
                    if b:
                        last = act.activation(probsT[n % 2][:, 512:768], bank[6][:, 0:256], ACT.Copy)
                    last.then_inc(probsT_ready, 1)
                if s < STEPS:
                    _, b, _ = step_of(s)
                    lo = HD if b else P
                    act.wait_ge(negmax_ready, s + 1)
                    for r in range(REP):
                        row = probs[s % 2][:, r, lo:]
                        act.activation(row, row, ACT.Exp, bias=neg_max[s % 2][:, r:r + 1],
                                       accum_out=denom[s % 2][:, r:r + 1])
                    act.activation(sink_e[s % 2], sink_e[s % 2], ACT.Exp).then_inc(exp_done, 1)

            split_hi(0)
            for c in range(ZV, Q):
                start_unit(c)
                for t in range(TT if c % 2 else 0):
                    a = 4 * (c // 2) + t
                    act.wait_ge(act_tile_done, a + 1)
                    if a == 0:
                        act.wait_ge(xnT_ready, KT)
                    act.activation(v_tok[:, t, (c // 2) * 512:(c // 2 + 1) * 512], bank[t][:, :],
                                   ACT.Gelu).then_inc(act_tile_read, 1)
            for c in range(Q, ZU):
                start_unit(c)
                for m in range(2):
                    j = 2 * (c - Q) + m
                    act.wait_ge(act_tile_done, 8 + j + 1)
                    if j == 0:
                        act.wait_ge(wsT_psum, 1)
                    dst = qT[:, j, :] if j < 8 else kT[:, j - 8, :] if j < 10 else vaT[:, j - 10, :]
                    act.activation(dst, bank[j % 2][:, :], ACT.Copy).then_inc(act_tile_read, 1)
            for c in range(ZU, GA):
                start_unit(c)
                for m in range(2):
                    g = 2 * (c - ZU) + m
                    gate_tile(20 + g, ACT.Gelu)
                    if g >= 5:
                        attention_slot(g - 5)
            for u in range(4):
                start_unit(GA + 2 * u)
                for m in range(2):
                    j = 2 * u + m
                    gate_tile(28 + j, ACT.Tanh, bias=gate_b[:, j:j + 1], scale=0.5)
                    attention_slot(3 + 4 * u + m)
                start_unit(GA + 2 * u + 1)
                for m in range(2):
                    attention_slot(5 + 4 * u + m)
            for u in range(4):
                start_unit(GB + 2 * u)
                for m in range(2):
                    j = 2 * u + m
                    gate_tile(36 + j, ACT.Tanh, bias=gate_b[:, KT + j:KT + j + 1], scale=0.5)
                start_unit(GB + 2 * u + 1)
            act.wait_ge(merged_ready, KT)
            act.dma_start(h_tok[:, :, :], x[0].rearrange("(t p) d -> p t d", p=P)).then_inc(x_reloaded, 16)
            late = [(ffn_g[:, :], norm_ffn_g[0].partition_broadcast(P)),
                    (w_router[:, :, 0:NG], w_router_group[0].rearrange("(p c) n -> p c n", p=P)),
                    (w_router[:, :, NG:NR], w_router_expert[0].rearrange("(p c) n -> p c n", p=P)),
                    (b_router[0:NG, :], b_router_group[0].rearrange("(p a) -> p a", a=1)),
                    (b_router[NG:NR, :], b_router_expert[0].rearrange("(p a) -> p a", a=1))]
            for dst, src in late:
                act.dma_start(dst, src).then_inc(late_loaded, 16)
            for c in range(WO, UNITS):
                start_unit(c)
            for t in range(TT):
                act.wait_ge(h_ready, TT + t + 1)
                act.wait_ge(hsq_summed, t)
                act.activation(squares[:, :], h_tok[:, t, :], ACT.Square, scale=float(D) ** -0.5,
                               accum_out=mean_sq[:, t:t + 1]).then_inc(hsq_summed, 1)
            for t in range(TT):
                act.wait_ge(hnT_psum, t + 1)
                act.activation(hnT[:, 0:4, t * P:(t + 1) * P],
                               bank[4 + 2 * (t % 2)][:, :].rearrange("p (c q) -> p c q", c=4),
                               ACT.Copy).then_inc(hnT_a, 1)
            for t in range(TT):
                act.wait_ge(hn_ready, t + 1)
                act.activation(hn_part[0][:, t, :, :], hn[:, t, :, :], ACT.Copy).then_inc(part0_ready, 1)
            for t in range(TT):
                act.wait_ge(rest_ready, t + 1)
                act.activation(hn_part[1][:, t, :, :], hn_rest[:, t, :, :], ACT.Copy).then_inc(part1_ready, 1)
            act.wait_ge(route_sub, 1)
            act.activation(gsel[:, :, :], gsel[:, :, :], ACT.Exp).then_inc(route_exp, 1)
            act.wait_ge(route_sub, 2)
            act.activation(r4[5], r4[5], ACT.Exp).then_inc(route_exp, 1)

            def copy_pack(i):
                act.wait_ge(pack_done, i + 1)
                act.activation(packT[:, 0:4, :], bank[2][:, :].rearrange("p (c q) -> p c q", c=4),
                               ACT.Copy).then_inc(pack_a, 1)

            def expert_pair(i):
                act.wait_ge(gate_done, i + 1)
                act.activation(silu_g[:, :], bank[0][:, :], ACT.Silu).then_inc(silu_ready, 1)
                copy_pack(i + 1)
                act.wait_ge(rows_turned, i + 1)
                act.activation(actT[:, :, :], bank[4][:, :].rearrange("p (c q) -> p c q", c=FT),
                               ACT.Copy).then_inc(actT_ready, 1)
                act.wait_ge(y_right, i + 1)
                act.activation(y_rows[:, 512:1024], bank[6][:, :], ACT.Copy).then_inc(y_right_ready, 1)
                act.wait_ge(y_left_ready, i + 1)
                act.wait_ge(y_right_ready, i + 1)
                act.dma_start(packed_y[bass.ds(i * P, P), :], y_rows[:, :]).then_inc(y_stored, 16)
                act.wait_ge(y_stored, 16 * i + 16)

            act.wait_ge(h_ready, 8)
            copy_pack(0)
            with act.Fori(0, PAIRS) as i:
                expert_pair(i)
            n_over = act.value_load(ov_count[0:1, 0:1], min_val=0, max_val=OV_TILES)
            with act.If(n_over > 0):
                with act.Fori(PAIRS, PAIRS + OV_PAIRS) as i:
                    expert_pair(i)
            act.dma_start(final_g[:, :], norm_final_g.partition_broadcast(P)).then_inc(late_loaded, 16)
            for t in range(TT):
                act.wait_ge(dve_final, t + 1)
                act.wait_ge(ysq_summed, t)
                act.activation(squares[:, :], h_tok[:, t, :], ACT.Square, scale=float(D) ** -0.5,
                               accum_out=mean_sq[:, t:t + 1]).then_inc(ysq_summed, 1)

        @block.vector
        def _(dve):
            steps = [0]

            def then(instruction):
                instruction.then_inc(dve_step, 1)
                steps[0] += 1
                dve.wait_ge(dve_step, steps[0])

            def inverse_root(y, value):
                then(dve.tensor_scalar(value, value, EPS, None, ALU.add))
                then(dve.tensor_scalar(y.bitcast(I32), value.bitcast(I32), -0.5, float(0x5F3759DF), ALU.mult, ALU.add))
                for _ in range(4):
                    work = root_work[:, 0:y.shape[1]]
                    then(dve.tensor_tensor(work, y, value, ALU.mult))
                    then(dve.scalar_tensor_tensor(out=work, in0=work, scalar=-0.5, in1=y, op0=ALU.mult, op1=ALU.mult))
                    then(dve.scalar_tensor_tensor(out=y, in0=work, scalar=1.5, in1=y, op0=ALU.add, op1=ALU.mult))

            dve.memset(ones_row[:, :], 1.0)
            dve.memset(probs[0][:, :, 0:HD], 0.0)
            dve.memset(probs[1][:, :, 0:HD], 0.0)
            dve.wait_ge(square_summed, TT)
            inverse_root(rstd, mean_sq)
            for t in range(TT):
                dve.tensor_scalar(xn_tok[:, t, :], x_tok[:, t, :], rstd[:, t:t + 1], None, ALU.mult).then_inc(normed, 1)
            dve.wait_ge(consts_loaded, 16 * 7)
            dve.wait_ge(vecs_psum, 1)
            then(dve.tensor_copy(small[:, 0:3 * KT], bank[7][:, 0:3 * KT]))
            for k in range(KT + 1):
                if k < KT:
                    dve.wait_ge(xnT_psum, k + 1)
                    dve.tensor_scalar(xg[:, k, :], bank[k % 4][:, :], mix_g[:, k:k + 1], None, ALU.mult).then_inc(xg_ready, 1)
                if k >= 1:
                    dve.wait_ge(xhi_ready, k)
                    dve.wait_ge(xg_ready, k)
                    dve.tensor_tensor(xnT_lo[:, k - 1, :], xg[:, k - 1, :], xnT_hi[:, k - 1, :].bitcast(F32),
                                      ALU.subtract).then_inc(xnT_ready, 1)

            def split_lo(c):
                dve.wait_ge(hi_split, c + 1)
                dve.tensor_tensor(wlo[c % 2][:, :], raw[c % 2][:, :], whi[c % 2][:, :].bitcast(F32),
                                  ALU.subtract).then_inc(lo_split, 1)

            def start_unit(c):
                if c + 1 < UNITS:
                    split_lo(c + 1)

            def make_alibi():
                dve.wait_ge(iota_made, 1)
                then(dve.tensor_copy(dist[:, :], dist_i[:, :]))
                then(dve.scalar_tensor_tensor(out=dist[:, :], in0=dist[:, :], scalar=-1.0, in1=dist[:, :],
                                              op0=ALU.mult, op1=ALU.max))
                then(dve.memset(band_mask[:, :], 0.0))
                dve.memset(band_mask[0:HD, 2 * HD:BAND], MASKED)
                then(dve.memset(band_mask[HD:P, 0:HD], MASKED))
                for h in range(H):
                    last = dve.scalar_tensor_tensor(out=alibi[:, h, :], in0=dist[:, :], scalar=-slopes[h],
                                                    in1=band_mask[:, :], op0=ALU.mult, op1=ALU.add)
                last.then_inc(alibi_ready, 1)
                then(dve.tensor_scalar(gate_b, gate_b, 0.5, None, ALU.mult))

            def layernorm_stats():
                for t in range(TT):
                    dve.wait_ge(act_tile_read, 4 + t + 1)
                    for n in range(2):
                        last = dve.bn_stats(ln_stats[:, t * 12 + n * 6:t * 12 + (n + 1) * 6],
                                            v_tok[:, t, n * 512:(n + 1) * 512])
                    then(last)
                    then(dve.bn_aggr(ln_mv[:, 2 * t:2 * t + 2], ln_stats[:, t * 12:(t + 1) * 12]))
                then(dve.tensor_copy(mean_sq, ln_mv.rearrange("p (t s) -> p t s", s=2)[:, :, 1]))
                inverse_root(rstd, mean_sq)

            def layernorm(t):
                row = v_tok[:, t, :]
                then(dve.tensor_scalar(row, row, ln_mv[:, 2 * t:2 * t + 1], rstd[:, t:t + 1], ALU.subtract, ALU.mult))
                then(dve.tensor_tensor(row, row, ln_g[:, :], ALU.mult))
                dve.tensor_tensor(row, row, ln_b[:, :], ALU.add).then_inc(ln_ready, 1)

            def attention_slot(s):
                if 1 <= s < STEPS + 1:
                    n = s - 1
                    _, b, _ = step_of(n)
                    lo = HD if b else P
                    dve.wait_ge(exp_done, n + 1)
                    then(dve.tensor_tensor(denom[n % 2], denom[n % 2], sink_e[n % 2], ALU.add))
                    then(dve.reciprocal(denom[n % 2], denom[n % 2]))
                    p = probs[n % 2][:, :, lo:]
                    dve.tensor_tensor(p, p, denom[n % 2].unsqueeze(2).to_broadcast([P, REP, 2 * P - lo]),
                                      ALU.mult).then_inc(probs_ready, 1)
                if s < STEPS:
                    pair, b, side = step_of(s)
                    kv = 2 * pair + side
                    skip = 0 if b else HD
                    if s == 0:
                        dve.wait_ge(alibi_ready, 1)
                    dve.wait_ge(scores_done, s + 1)
                    if s >= 2:
                        dve.wait_ge(turned, s - 1)
                    for r in range(0, REP, 2):
                        last = dve.scalar_tensor_tensor(
                            out=probs[s % 2][:, r:r + 2, HD + skip:],
                            in0=bank[3 + r // 2][:, 0:2 * BAND].rearrange("p (r k) -> p r k", r=2)[:, :, skip:],
                            scalar=SCALE, in1=alibi[:, REP * kv + r:REP * kv + r + 2, skip:], op0=ALU.mult, op1=ALU.add)
                    last.then_inc(scores_read, 1)
                    dve.wait_ge(scores_read, s + 1)
                    sink = sinks[:, REP * kv:REP * (kv + 1)]
                    then(dve.tensor_reduce(neg_max[s % 2], probs[s % 2][:, :, HD + skip:], AX.X, ALU.max))
                    then(dve.tensor_tensor(neg_max[s % 2], neg_max[s % 2], sink, ALU.max))
                    then(dve.tensor_scalar(neg_max[s % 2], neg_max[s % 2], -1.0, None, ALU.mult))
                    dve.tensor_tensor(sink_e[s % 2], sink, neg_max[s % 2], ALU.add).then_inc(negmax_ready, 1)
                if s >= 4 and s % 2 == 0:
                    n = s - 3
                    pair, b, _ = step_of(n)
                    dve.wait_ge(pv_done, n // 2 + 1)
                    src = bank[7][:, :].rearrange("p (r q) -> p r q", q=P)
                    hi = attT_hi[:, pair * REP:(pair + 1) * REP, b * P:(b + 1) * P]
                    lo = attT_lo[:, pair * REP:(pair + 1) * REP, b * P:(b + 1) * P]
                    then(dve.tensor_copy(hi, src))
                    dve.tensor_tensor(lo, src, hi.bitcast(F32), ALU.subtract).then_inc(att_ready, 1)

            split_lo(0)
            for c in range(ZV, Q):
                start_unit(c)
                if c == 0:
                    make_alibi()
                if c == 1:
                    dve.wait_ge(wsT_psum, 1)
                    for g4 in range(2):
                        last = dve.tensor_copy(wsT[:, 4 * g4:4 * g4 + 4, :],
                                               bank[6 + g4][:, :].rearrange("p (g i) -> p g i", g=4))
                    then(last)
                    dve.memset(wsT[HD:P, :, 0:HD], 0.0).then_inc(wsT_ready, 1)
            for c in range(Q, ZU):
                start_unit(c)
                if c == Q:
                    layernorm_stats()
                if c - Q < TT:
                    layernorm(c - Q)
            for c in range(ZU, GA):
                start_unit(c)
                for m in range(2):
                    g = 2 * (c - ZU) + m
                    if g == 0:
                        dve.wait_ge(va_psum, 1)
                        for j in range(2):
                            last = dve.tensor_copy(va_tok[:, :, j * P:(j + 1) * P],
                                                   bank[6 + j][:, :].rearrange("p (t c) -> p t c", t=TT))
                        last.then_inc(va_ready, 1)
                    dve.wait_ge(sv_done, g + 1)
                    dve.wait_ge(act_tile_read, 20 + g + 1)
                    dve.wait_ge(sp_ready, g)
                    dve.tensor_tensor(gated[:, :], gbuf[g % 2][:, :], bank[2][:, :], ALU.mult).then_inc(gate_used, 1)
                    dve.wait_ge(gate_used, g + 1)
                    then(dve.tensor_copy(spT_hi[:, g, :], gated[:, :]))
                    dve.tensor_tensor(spT_lo[:, g, :], gated[:, :], spT_hi[:, g, :].bitcast(F32),
                                      ALU.subtract).then_inc(sp_ready, 1)
                    if g >= 5:
                        attention_slot(g - 5)
            for u in range(4):
                start_unit(GA + 2 * u)
                for m in range(2):
                    attention_slot(3 + 4 * u + m)
                start_unit(GA + 2 * u + 1)
                for m in range(2):
                    d = 2 * u + m
                    dve.wait_ge(dve_tile_done, d + 1)
                    dve.wait_ge(act_tile_read, 28 + d + 1)
                    dve.scalar_tensor_tensor(out=branch_a[:, d, :], in0=gbuf[d % 2][:, :], scalar=1.0, in1=bank[2][:, :],
                                             op0=ALU.add, op1=ALU.mult).then_inc(gate_used, 1)
                    attention_slot(5 + 4 * u + m)
            for u in range(4):
                start_unit(GB + 2 * u)
                start_unit(GB + 2 * u + 1)
                for m in range(2):
                    j = 2 * u + m
                    dve.wait_ge(dve_tile_done, 8 + j + 1)
                    dve.wait_ge(act_tile_read, 36 + j + 1)
                    dve.wait_ge(merged_ready, j)
                    dve.scalar_tensor_tensor(out=merged[:, :], in0=gbuf[j % 2][:, :], scalar=1.0, in1=bank[2 + j % 2][:, :],
                                             op0=ALU.add, op1=ALU.mult).then_inc(gate_used, 1)
                    dve.wait_ge(gate_used, 16 + j + 1)
                    then(dve.tensor_tensor(merged[:, :], merged[:, :], branch_a[:, j, :], ALU.add))
                    then(dve.tensor_scalar(mgT_hi[:, j, :], merged[:, :], 0.5, None, ALU.mult))
                    dve.scalar_tensor_tensor(out=mgT_lo[:, j, :], in0=merged[:, :], scalar=0.5,
                                             in1=mgT_hi[:, j, :].bitcast(F32), op0=ALU.mult,
                                             op1=ALU.subtract).then_inc(merged_ready, 1)
            for c in range(WO, UNITS):
                start_unit(c)
                for t in range(TT if c % 2 else 0):
                    n = (c - WO) // 2
                    dve.wait_ge(x_reloaded, 16)
                    dve.wait_ge(dve_tile_done, 16 + 4 * n + t + 1)
                    part = h_tok[:, t, n * 512:(n + 1) * 512]
                    dve.tensor_tensor(part, bank[t][:, :], part, ALU.add).then_inc(h_ready, 1)

            dve.wait_ge(late_loaded, 16 * 5)
            dve.wait_ge(h_ready, 8)
            dve.wait_ge(hsq_summed, TT)
            inverse_root(rstd, mean_sq)
            for t in range(TT):
                dve.scalar_tensor_tensor(out=hn[:, t, :, :].rearrange("q c p -> q p c"),
                                         in0=h_tok[:, t, :].rearrange("q (p c) -> q p c", c=KT),
                                         scalar=rstd[:, t:t + 1], in1=ffn_g[:, :].rearrange("q (p c) -> q p c", c=KT),
                                         op0=ALU.mult, op1=ALU.mult).then_inc(hn_ready, 1)
            for t in range(TT):
                dve.wait_ge(hnT_psum, t + 1)
                dve.tensor_copy(hnT[:, 4:8, t * P:(t + 1) * P],
                                bank[5 + 2 * (t % 2)][:, :].rearrange("p (c q) -> p c q", c=4)).then_inc(hnT_b, 1)
            dve.wait_ge(hn_ready, TT)
            for t in range(TT):
                dve.wait_ge(part0_ready, t + 1)
                dve.tensor_tensor(hn_rest[:, t, :, :], hn[:, t, :, :], hn_part[0][:, t, :, :],
                                  ALU.subtract).then_inc(rest_ready, 1)
            dve.wait_ge(rest_ready, TT)
            for t in range(TT):
                dve.wait_ge(part1_ready, t + 1)
                dve.tensor_tensor(hn_part[2][:, t, :, :], hn_rest[:, t, :, :], hn_part[1][:, t, :, :],
                                  ALU.subtract).then_inc(part2_ready, 1)

            dve.wait_ge(logitsT_done, 1)
            dve.tensor_scalar(logitsT[:, :], bank[0][0:NR, :], b_router[:, 0:1], None, ALU.add).then_inc(logitsT_ready, 1)
            dve.wait_ge(logits_turned, 1)
            then(dve.tensor_copy(logits[:, :, :], bank[1][:, 0:TT * NR].rearrange("p (t n) -> p t n", t=TT)))
            dve.wait_ge(route_iotas_made, 6)
            glog, elog = logits[:, :, 0:NG], logits[:, :, NG:NR]
            gmax, best, p_group, v1, v2, gap = r4[:6]

            def wide_t(a, n):
                return a.unsqueeze(2).to_broadcast([P, TT, n])

            def wide_e(a, n=NE):
                return a[:, 0:n].unsqueeze(1).to_broadcast([P, TT, n])

            def first_of(values, top, chosen, work, n):
                then(dve.tensor_tensor(work, values, wide_t(top, n), ALU.is_equal))
                then(dve.tensor_scalar(work, work, -64.0, None, ALU.mult))
                then(dve.tensor_tensor(work, work, wide_e(expert_iota, n), ALU.add))
                then(dve.tensor_reduce(best, work, AX.X, ALU.min))
                then(dve.tensor_tensor(chosen, work, wide_t(best, n), ALU.is_equal))

            then(dve.tensor_reduce(gmax, glog, AX.X, ALU.max))
            dve.tensor_tensor(gsel[:, :, :], glog, wide_t(gmax, NG), ALU.subtract).then_inc(route_sub, 1)
            dve.wait_ge(route_exp, 1)
            then(dve.tensor_reduce(p_group, gsel[:, :, :], AX.X, ALU.add))
            then(dve.reciprocal(p_group, p_group))
            first_of(glog, gmax, gsel[:, :, :], gcand[:, :, :], NG)
            then(dve.tensor_scalar(gcand[:, :, :], gsel[:, :, :], -1.0, -MASKED, ALU.add, ALU.mult))
            for t in range(TT):
                by_group = lambda a: a[:, t, :].rearrange("p (g e) -> p g e", g=NG)
                over = lambda a: a[:, t, :].unsqueeze(2).to_broadcast([P, NG, EPG])
                then(dve.tensor_tensor(by_group(em), elog[:, t, :].rearrange("p (g e) -> p g e", g=NG), over(gsel), ALU.mult))
                then(dve.tensor_tensor(by_group(em), by_group(em), over(gcand), ALU.add))
            then(dve.tensor_reduce(v1, em[:, :, :], AX.X, ALU.max))
            first_of(em[:, :, :], v1, sel_a[:, :, :], cand[:, :, :], NE)
            then(dve.scalar_tensor_tensor(out=em[:, :, :], in0=sel_a[:, :, :], scalar=2 * MASKED, in1=em[:, :, :],
                                          op0=ALU.mult, op1=ALU.add))
            then(dve.tensor_reduce(v2, em[:, :, :], AX.X, ALU.max))
            dve.tensor_tensor(gap, v2, v1, ALU.subtract).then_inc(route_sub, 1)
            first_of(em[:, :, :], v2, sel_b[:, :, :], cand[:, :, :], NE)
            dve.tensor_tensor(picked[:, :, :], sel_a[:, :, :], sel_b[:, :, :], ALU.add).then_inc(picked_ready, 1)
            dve.wait_ge(route_exp, 2)
            then(dve.tensor_scalar(v1, gap, 1.0, None, ALU.add))
            then(dve.reciprocal(v1, v1))
            then(dve.tensor_tensor(w_first, v1, p_group, ALU.mult))
            then(dve.tensor_tensor(w_second, gap, w_first, ALU.mult))
            dve.wait_ge(ranks_done, 1)
            dve.tensor_copy(rank[:, :, :], bank[2][:, 0:TT * NE].rearrange("p (t e) -> p t e", t=TT))
            then(dve.tensor_copy(counts[:, :], bank[3][:, 0:NE]))
            then(dve.tensor_scalar(tiles_ov[:, :], counts[:, :], float(ROWS), None, ALU.is_gt))
            for j in range(2, MAX_OV + 1):
                then(dve.scalar_tensor_tensor(out=tiles_ov[:, :], in0=counts[:, :], scalar=float(ROWS * j),
                                              in1=tiles_ov[:, :], op0=ALU.is_gt, op1=ALU.add))
            then(dve.tensor_copy(scan_a[:, :], tiles_ov[:, :]))
            src, dst, shift = scan_a, scan_b, 1
            while shift < NE:
                dve.tensor_copy(dst[:, 0:shift], src[:, 0:shift])
                then(dve.tensor_tensor(dst[:, shift:], src[:, shift:], src[:, 0:NE - shift], ALU.add))
                src, dst, shift = dst, src, 2 * shift
            sums = src
            then(dve.tensor_tensor(delta[:, :], sums[:, :], tiles_ov[:, :], ALU.subtract))
            then(dve.tensor_scalar(delta[:, :], delta[:, :], float(ROWS), float(ROWS * (NE - 1)), ALU.mult, ALU.add))
            then(dve.tensor_tensor(delta[:, :], delta[:, :], first_row[:, :], ALU.subtract))
            then(dve.tensor_scalar(cand[:, :, :], rank[:, :, :], float(ROWS), None, ALU.is_ge))
            then(dve.tensor_tensor(cand[:, :, :], cand[:, :, :], wide_e(delta), ALU.mult))
            then(dve.tensor_tensor(rank[:, :, :], rank[:, :, :], cand[:, :, :], ALU.add))
            then(dve.tensor_tensor(rank[:, :, :], rank[:, :, :], wide_e(first_row), ALU.add))
            for chosen, rows in ((sel_a, row_first), (sel_b, row_second)):
                then(dve.tensor_tensor(cand[:, :, :], chosen[:, :, :], rank[:, :, :], ALU.mult))
                then(dve.tensor_reduce(rows, cand[:, :, :], AX.X, ALU.add))
            dve.tensor_copy(rows_i[:, 0:TT], row_first)
            then(dve.tensor_copy(rows_i[:, TT:2 * TT], row_second))

            def make_onehot(i):
                for t in range(TT):
                    dve.tensor_scalar(onehot_half[:, t, :], row_iota[:, :], row_first[:, t:t + 1], None,
                                      ALU.is_equal).then_inc(half_onehot, 1)
                dve.wait_ge(half_onehot, 5 * i + TT)
                for t in range(TT):
                    last = dve.scalar_tensor_tensor(out=onehot[:, t, :], in0=row_iota[:, :], scalar=row_second[:, t:t + 1],
                                                    in1=onehot_half[:, t, :], op0=ALU.is_equal, op1=ALU.add)
                last.then_inc(onehot_ready, 1)
                dve.wait_ge(onehot_ready, i + 1)
                dve.tensor_scalar(row_first, row_first, -float(P), None, ALU.add)
                dve.tensor_scalar(row_second, row_second, -float(P), None, ALU.add).then_inc(half_onehot, 1)
                dve.wait_ge(half_onehot, 5 * i + 5)

            def copy_pack(i):
                dve.wait_ge(pack_done, i + 1)
                dve.tensor_copy(packT[:, 4:8, :], bank[3][:, :].rearrange("p (c q) -> p c q", c=4)).then_inc(pack_b, 1)

            make_onehot(0)
            then(dve.tensor_tensor(ov_cmp[:, :, :], sums[0:1, :].unsqueeze(1).to_broadcast([1, OV_TILES, NE]),
                                   ov_iota[:, :].unsqueeze(2).to_broadcast([1, OV_TILES, NE]), ALU.is_le))
            then(dve.tensor_reduce(ov_id[:, :], ov_cmp[:, :, :], AX.X, ALU.add))
            then(dve.tensor_scalar(ov_id[:, :], ov_id[:, :], float(NE - 1), None, ALU.min))
            then(dve.tensor_copy(ov_expert[:, :], ov_id[:, :]))
            dve.tensor_copy(ov_count[:, :], sums[0:1, NE - 1:NE]).then_inc(routed, 1)
            copy_pack(0)

            def expert_pair(i):
                make_onehot(i + 1)
                dve.wait_ge(silu_ready, i + 1)
                dve.wait_ge(up_done, i + 1)
                dve.tensor_tensor(act_rows[:, :, :].rearrange("q c p -> q p c"),
                                  silu_g[:, :].rearrange("q (p c) -> q p c", c=FT),
                                  bank[1][:, :].rearrange("q (p c) -> q p c", c=FT), ALU.mult).then_inc(rows_ready, 1)
                copy_pack(i + 1)
                dve.wait_ge(y_left, i + 1)
                dve.tensor_copy(y_rows[:, 0:512], bank[5][:, :]).then_inc(y_left_ready, 1)

            with dve.Fori(0, PAIRS) as i:
                expert_pair(i)
            n_over = dve.value_load(ov_count[0:1, 0:1], min_val=0, max_val=OV_TILES)
            with dve.If(n_over > 0):
                with dve.Fori(PAIRS, PAIRS + OV_PAIRS) as i:
                    expert_pair(i)

            for t in range(TT):
                dve.wait_ge(y_gathered[t], 32)
                h = h_tok[:, t, :]
                then(dve.scalar_tensor_tensor(out=h, in0=y_first[:, t, :], scalar=w_first[:, t:t + 1], in1=h,
                                              op0=ALU.mult, op1=ALU.add))
                dve.scalar_tensor_tensor(out=h, in0=y_second[:, t, :], scalar=w_second[:, t:t + 1], in1=h,
                                         op0=ALU.mult, op1=ALU.add).then_inc(dve_final, 1)
            dve.wait_ge(late_loaded, 16 * 6)
            for t in range(TT):
                dve.wait_ge(ysq_summed, t + 1)
                inverse_root(rstd[:, t:t + 1], mean_sq[:, t:t + 1])
                dve.scalar_tensor_tensor(out=result[:, t, :], in0=h_tok[:, t, :], scalar=rstd[:, t:t + 1],
                                         in1=final_g[:, :], op0=ALU.mult, op1=ALU.mult).then_inc(result_ready, 1)


_INS = ["x", "norm_mix_g", "w_in", "gate_bias", "gmlp_ln_g", "gmlp_ln_b", "gmlp_w_s", "gmlp_b_s",
        "attn_sinks", "w_branch_a", "w_branch_b", "w_out", "norm_ffn_g", "w_router_group",
        "b_router_group", "w_router_expert", "b_router_expert", "w_gate", "w_up", "w_down",
        "norm_final_g"]


def kernel(**inputs):
    import concourse.bacc as bacc
    from concourse.bass_utils import run_bass_kernel_spmd

    nc = bacc.Bacc("TRN2", target_bir_lowering=False, num_devices=1, dynamic_dma_scratch_size=4096)
    arrays, args = {}, []
    for name in _INS:
        a = np.ascontiguousarray(inputs[name])
        arrays[name] = a
        args.append(nc.dram_tensor(name, a.shape, mybir.dt.from_np(a.dtype), kind="ExternalInput").ap())
    shape = arrays["x"].shape
    args.append(nc.dram_tensor("out", shape, F32, kind="ExternalOutput").ap())
    build_block(nc, *args)
    got = run_bass_kernel_spmd(nc, [arrays], core_ids=[0])
    return got.results[0]["out"]
```

```python
from contextlib import ExitStack

import numpy as np

import concourse.bass as bass
from concourse import mybir

F32 = mybir.dt.float32
F32R = mybir.dt.float32r
BF16 = mybir.dt.bfloat16
I32 = mybir.dt.int32
ALU = mybir.AluOpType
ACT = mybir.ActivationFunctionType
AX = mybir.AxisListType

P = 128
EPS = 1e-6
MASKED = -1e30
FAR = 8192.0
KB = 1024


def build_block(nc, x, norm_mix_g, w_in, gate_bias, gmlp_ln_g, gmlp_ln_b, gmlp_w_s, gmlp_b_s,
                attn_sinks, w_branch_a, w_branch_b, w_out, norm_ffn_g, w_router_group,
                b_router_group, w_router_expert, b_router_expert, w_gate, w_up, w_down,
                norm_final_g, out):
    _, SEQ, D = x.shape
    TT = SEQ // P
    KT = D // P
    GROUPS = gmlp_w_s.shape[1]
    H = attn_sinks.shape[1]
    KVW = (w_in.shape[2] - 5 * D) // 2
    HD = D // H
    KVH = KVW // HD
    REP = H // KVH
    BAND = P + HD
    NG = w_router_group.shape[2]
    NE = w_router_expert.shape[2]
    EPG = NE // NG
    DE = w_gate.shape[3]
    FT = DE // P
    ROWS = 64
    PAIRS = NE // 2
    OV_PAIRS = -(-((2 * SEQ - NE) // ROWS) // 2)
    OV_TILES = 2 * OV_PAIRS
    FAR_PAIRS = PAIRS - 6
    MAX_OV = SEQ // ROWS - 1
    NR = NG + NE
    SCALE = float(HD) ** -0.5
    slopes = [float(np.float32(2.0 ** (-8.0 * (h + 1) / H))) for h in range(H)]
    assert PAIRS % 2 == OV_PAIRS % 2 == 0
    assert GROUPS == KT == 8 and TT == 4 and KVH == 4 and REP == 4 and HD == ROWS == 64 and FT == 4

    base = -(-nc.sbuf_base // 64) * 64

    def at(name, shape, dt, kb):
        return nc.alloc_sbuf_tensor_at(name, shape, dt, offset=base + int(kb * KB))

    xnT_hi = at("xnT_hi", [P, KT, SEQ], F32R, 0)
    xnT_lo = at("xnT_lo", [P, KT, SEQ], F32R, 16)
    v_tok = at("v_tok", [P, TT, D], F32, 32)
    attT_hi = at("attT_hi", [P, KT, SEQ], F32R, 32)
    attT_lo = at("attT_lo", [P, KT, SEQ], F32R, 48)
    dist_i = at("dist_i", [P, BAND], I32, 48)
    dist = at("dist", [P, BAND], F32, 49)
    band_mask = at("band_mask", [P, BAND], F32, 50)
    gated = at("gated", [P, SEQ], F32, 52)
    ws_nat = at("ws_nat", [P, GROUPS, P], F32, 64)
    qT = at("qT", [P, KT, SEQ], F32, 64)
    ln_g = at("ln_g", [P, D], F32, 80)
    ln_b = at("ln_b", [P, D], F32, 84)
    vaT = at("vaT", [P, 2, SEQ], F32, 88)
    gate_bs = at("gate_bs", [P, GROUPS, P], F32, 92)
    branch_a = at("branch_a", [P, KT, SEQ], F32, 80)
    x_tok = at("x_tok", [P, TT, D], F32, 96)
    xn_tok = at("xn_tok", [P, TT, D], F32, 112)
    spT_hi = at("spT_hi", [P, KT, SEQ], F32R, 96)
    spT_lo = at("spT_lo", [P, KT, SEQ], F32R, 112)
    mgT_hi = at("mgT_hi", [P, KT, SEQ], F32R, 96)
    mgT_lo = at("mgT_lo", [P, KT, SEQ], F32R, 112)
    raw = [at(f"raw{b}", [P, 2048], F32, 128 + 8 * b) for b in range(2)]
    whi = [at(f"whi{b}", [P, 2048], F32R, 144 + 8 * b) for b in range(2)]
    wlo = [at(f"wlo{b}", [P, 2048], F32R, 160 + 8 * b) for b in range(2)]
    kT = at("kT", [P, 2, SEQ], F32, 176)
    va_tok = at("va_tok", [P, TT, KVW], F32, 180)
    probs = [at(f"probs{b}", [P, REP, 2 * P], F32, 184 + 4 * b) for b in range(2)]
    probsT = [at(f"probsT{b}", [P, 768], F32, 192 + 3 * b) for b in range(2)]
    merged = at("merged", [P, SEQ], F32, 192)
    wsT = at("wsT", [P, GROUPS, P], F32, 198)
    alibi = at("alibi", [P, H, BAND], F32, 202)
    gbuf = [at(f"gbuf{b}", [P, SEQ], F32, 214 + 2 * b) for b in range(2)]
    vec_rows = at("vec_rows", [3 * KT, P], F32, 214)
    ident = at("ident", [P, P], F32, 218)
    small = at("small", [P, 204], F32, 218.5)
    W = [at(f"W{u}", [P, 8 * DE], F32, kb) for u, kb in enumerate((0, 16, 32, 48, 64, 80, 160, 144, 128))]
    hn_part = [at(f"hn_part{j}", [P, TT, KT, P], BF16, 96 + 8 * j) for j in range(3)]
    packT = at("packT", [P, KT, P], F32, 120)
    y_hi = at("y_hi", [P, D], F32R, 124)
    hg = at("hg", [P, TT, KT, P], F32, 128)
    hgT = [at(f"hgT{j}", [P, KT, 2 * P], F32, 144 + 8 * j) for j in range(2)]
    hn_rest = hg
    h_tok = at("h_tok", [P, TT, D], F32, 176)
    ffn_g = at("ffn_g", [P, D], F32, 192)
    w_router = at("w_router", [P, KT, P // 2], F32, 196)
    logitsT = at("logitsT", [P, SEQ], F32, 214)
    squares = at("squares", [P, 512], F32, 216)
    logits = at("logits", [P, TT, NR], F32, 198)
    b_router = at("b_router", [P, NR], F32, 198.5625)
    silu_g = at("silu_g", [P, DE], F32, 200)
    act_rows = at("act_rows", [P, FT, P], F32, 202)
    actT = at("actT", [P, FT, P], F32, 204)
    onehot = at("onehot", [P, TT, P], BF16, 206)
    weight_a = at("weight_a", [P, TT, P], F32, 214)
    weight_b = at("weight_b", [P, TT, P], F32, 216)
    y_lo = at("y_lo", [P, D], F32R, 192)
    onehotT = at("onehotT", [P, SEQ], F32R, 196)
    row_iota = at("row_iota", [P, P], F32, 207.5)
    final_g = at("final_g", [P, D], F32, 208)
    result = at("result", [P, TT, D], F32, 32)

    taken = [0]

    def col(n):
        taken[0] += n
        assert taken[0] <= 204
        return small[:, taken[0] - n:taken[0]]

    mix_g, gate_b, sinks = col(KT), col(2 * KT), col(H)
    mean_sq, rstd, root_work = col(TT), col(TT), col(TT)
    ln_stats, ln_mv = col(TT * 12), col(TT * 2)
    neg_max, sink_e, denom = ([col(REP) for _ in range(2)] for _ in range(3))
    w_first, w_second, row_first, row_second = col(TT), col(TT), col(TT), col(TT)
    row_weight = col(1)
    half_sq = ln_stats[:, 0:2 * TT]

    room = [208.0]

    def temp(name, shape, dt=F32):
        n = int(np.prod(shape[1:])) * 4 / KB
        room[0] += n
        assert room[0] <= 214
        return at(name, shape, dt, room[0] - n)

    em, sel_a, sel_b, cand, rank, beyond = (temp(f"route{i}", [P, TT, NE]) for i in range(6))
    picked = temp("picked", [P, TT, NE], BF16)
    expert_iota = temp("expert_iota", [P, NE])
    first_row = temp("first_row", [P, NE])
    tiles_ov, scan_a, scan_b, delta = (temp(f"route_e{i}", [P, NE]) for i in range(4))
    route_t = temp("route_t", [P, 8 * TT])
    r4 = [route_t[:, i * TT:(i + 1) * TT] for i in range(8)]
    gsel, gcand, gexp = (temp(n, [P, TT, NG]) for n in ("gsel", "gcand", "gexp"))
    earlier = at("earlier", [P, P], BF16, 199)
    all_ones = at("all_ones", [P, P], BF16, 199.25)
    tile_ends = at("tile_ends", [P, NE, MAX_OV], F32, 202)
    over_end = at("over_end", [P, NE, MAX_OV], F32, 204)
    ov_iota = at("ov_iota", [1, OV_TILES], F32, 199.5)
    ov_cmp = at("ov_cmp", [1, OV_TILES, NE], F32, 202)
    ov_id = at("ov_id", [1, OV_TILES], F32, 199.5625)
    ov_expert = at("ov_expert", [1, OV_TILES], I32, 199.625)
    ov_count = at("ov_count", [1, 1], I32, 199.6875)

    ctx = ExitStack()
    with ctx:
        bank = [ctx.enter_context(nc.psum_tensor(f"bank{i}", [P, 512], F32)) for i in range(8)]

        def sem(name):
            return ctx.enter_context(nc.semaphore(name))

        WIDE, TALL = 4, 8
        units = []

        def raw_view(c, kt):
            return raw[c % 2][:, :].rearrange("p (k n) -> p k n", k=kt)

        def add_unit(kt, moves):
            c = len(units)
            units.append([(dst(raw_view(c, kt)), src) for dst, src in moves])

        whole = lambda v: v
        for n in range(2):
            for kh in range(2):
                add_unit(WIDE, [(whole, w_in[0, kh * 512:(kh + 1) * 512, D + n * 512:D + (n + 1) * 512]
                                 .rearrange("(k p) n -> p k n", p=P))])
        for u in range(4):
            moves = []
            for m in range(2):
                for s in range(2):
                    head = 8 * (u // 2) + 4 * s + 2 * (u % 2) + m
                    moves.append((lambda v, m=m, s=s: v[:, :, m * P + s * HD:m * P + (s + 1) * HD],
                                  w_in[0, :, 2 * D + head * HD:2 * D + (head + 1) * HD]
                                  .rearrange("(k p) n -> p k n", p=P)))
            add_unit(TALL, moves)

        def tall(w, c0):
            add_unit(TALL, [(whole, w[:, c0:c0 + 256].rearrange("(k p) n -> p k n", p=P))])

        tall(w_in[0], 3 * D)
        tall(w_in[0], 3 * D + KVW)
        for u in range(4):
            tall(w_in[0], u * 256)
        for u in range(4):
            tall(w_in[0], 3 * D + 2 * KVW + u * 256)
            tall(w_branch_a[0], u * 256)
        for u in range(4):
            tall(w_in[0], 4 * D + 2 * KVW + u * 256)
            by_head = w_branch_b[0].rearrange("(p s r q) n -> s q p r n", p=2, s=2, r=REP, q=HD)
            moves = []
            for s in range(2):
                for pp in range(2):
                    moves.append((lambda v, s=s, pp=pp: v[s * HD:(s + 1) * HD, pp * REP:(pp + 1) * REP, :],
                                  by_head[s, :, pp, :, u * 256:(u + 1) * 256]))
            add_unit(TALL, moves)
        for n in range(2):
            for kh in range(2):
                add_unit(WIDE, [(whole, w_out[0, kh * 512:(kh + 1) * 512, n * 512:(n + 1) * 512]
                                 .rearrange("(k p) n -> p k n", p=P))])
        ZV, Q, KVA, ZU, GA, GB, WO = 0, 4, 8, 10, 14, 22, 30
        UNITS = len(units)
        landed = []
        for c in range(UNITS):
            landed.append((landed[c - 2] if c >= 2 else 0) + 16 * len(units[c]))

        x_loaded, x_reloaded = [sem(f"x_loaded{t}") for t in range(TT)], sem("x_reloaded")
        vecs_loaded = sem("vecs_loaded")
        consts_loaded, late_loaded = sem("consts_loaded"), sem("late_loaded")
        unit_loaded = [sem("unit_loaded0"), sem("unit_loaded1")]
        hi_split, lo_split = sem("hi_split"), sem("lo_split")
        half_used = sem("half_used")
        ident_made, iota_made, route_iotas_made = sem("ident_made"), sem("iota_made"), sem("route_iotas_made")
        vecs_psum = sem("vecs_psum")
        square_summed, vecs_ready, x_rstd_ready = sem("square_summed"), sem("vecs_ready"), sem("x_rstd_ready")
        normed_low, normed_high = sem("normed_low"), sem("normed_high")
        xnT_psum, xhi_ready, xnT_ready = (sem(n) for n in ("xnT_psum", "xhi_ready", "xnT_ready"))
        act_tile_done, act_tile_read = sem("act_tile_done"), sem("act_tile_read")
        dve_tile_done, gate_used = sem("dve_tile_done"), sem("gate_used")
        wsT_psum, wsT_ready, ln_ready = sem("wsT_psum"), sem("wsT_ready"), sem("ln_ready")
        va_psum, va_ready = sem("va_psum"), sem("va_ready")
        sv_done, sp_ready = sem("sv_done"), sem("sp_ready")
        alibi_ready, scores_done, scores_read, negmax_ready = (
            sem(n) for n in ("alibi_ready", "scores_done", "scores_read", "negmax_ready"))
        exp_done, probs_ready, turned, probsT_ready = (
            sem(n) for n in ("exp_done", "probs_ready", "turned", "probsT_ready"))
        pv_done, att_ready, merged_ready, h_ready = (
            sem(n) for n in ("pv_done", "att_ready", "merged_ready", "h_ready"))
        dve_step = sem("dve_step")
        hsq_summed, hg_ready, hgT_psum, hgT_a, hgT_b, rstd_ready = (
            sem(n) for n in ("hsq_summed", "hg_ready", "hgT_psum", "hgT_a", "hgT_b", "rstd_ready"))
        part0_ready, rest_ready, part1_ready, part2_ready = (
            sem(n) for n in ("part0_ready", "rest_ready", "part1_ready", "part2_ready"))
        logitsT_done, logitsT_ready, logits_turned = (
            sem(n) for n in ("logitsT_done", "logitsT_ready", "logits_turned"))
        route_sub, route_exp, picked_ready, ranks_done, routed = (
            sem(n) for n in ("route_sub", "route_exp", "picked_ready", "ranks_done", "routed"))
        w_loaded = [sem(f"w_loaded{u}") for u in range(9)]
        row_step, onehot_ready = sem("row_step"), sem("onehot_ready")
        pack_done, pack_a, pack_b = sem("pack_done"), sem("pack_a"), sem("pack_b")
        gate_half_done = sem("gate_half_done")
        gate_done, up_done, silu_ready, rows_ready, rows_turned, actT_ready = (
            sem(n) for n in ("gate_done", "up_done", "silu_ready", "rows_ready", "rows_turned", "actT_ready"))
        y_left, y_right, y_hi_ready, y_lo_ready = (sem(n) for n in ("y_left", "y_right", "y_hi_ready", "y_lo_ready"))
        weights_turned, row_weight_ready, onehotT_ready = (
            sem(n) for n in ("weights_turned", "row_weight_ready", "onehotT_ready"))
        spread_done, h_added = sem("spread_done"), sem("h_added")
        ysq_summed, final_gained, out_stored = sem("ysq_summed"), sem("final_gained"), sem("out_stored")
        y_rstd_ready = sem("y_rstd_ready")
        result_low, result_high = sem("result_low"), sem("result_high")
        hn_ready = sem("hn_ready")
        router_cleared, ranks_read, counts_read = sem("router_cleared"), sem("ranks_read"), sem("counts_read")
        h_final = sem("h_final")

        def wait_unit_used(eng, c):
            if c < Q:
                if c % 2 == 0:
                    eng.wait_ge(half_used, c // 2 + 1)
                else:
                    eng.wait_ge(act_tile_done, 4 * (c // 2 + 1))
            elif c < GA:
                eng.wait_ge(act_tile_done, 8 + 2 * (c - Q + 1))
            elif c < WO:
                if (c - GA) % 2 == 0:
                    eng.wait_ge(act_tile_done, 28 + (c - GA) + 2)
                else:
                    eng.wait_ge(dve_tile_done, (c - GA) + 1)
            elif c % 2 == 0:
                eng.wait_ge(half_used, 3 + (c - WO) // 2)
            else:
                eng.wait_ge(dve_tile_done, 16 + 4 * ((c - WO) // 2 + 1))

        SPREAD_BANKS = ((0, 1, 4, 7), (5, 6, 0, 1))

        STEPS = KVH * TT

        def step_of(n):
            return n // (2 * TT), (n // 2) % TT, n % 2

        block = ctx.enter_context(nc.Block())

        @block.sync
        def _(sp):
            def load_unit(c):
                if c >= 2:
                    sp.wait_ge(hi_split, c - 1)
                    sp.wait_ge(lo_split, c - 1)
                for dst, src in units[c]:
                    sp.dma_start(dst, src).then_inc(unit_loaded[c % 2], 16)

            def load_experts(u, w, e0, e1):
                for s, e in enumerate((e0, e1)):
                    sp.dma_start(W[u + s][:, :].rearrange("p (a n) -> p a n", a=1),
                                 w[0, bass.ds(e, 1), :, :].rearrange("a (p c) n -> p a (c n)", p=P)
                                 ).then_inc(w_loaded[u + s], 16)

            def load_down(e0, e1, used=None):
                for n, half_used_up in enumerate((y_left, y_right)):
                    if used is not None:
                        sp.wait_ge(half_used_up, used)
                    for s, e in enumerate((e0, e1)):
                        sp.dma_start(W[4 + s][:, :].rearrange("p (a c n) -> p a c n", a=1, c=FT)[:, :, :, n * 512:(n + 1) * 512],
                                     w_down[0, bass.ds(e, 1), :, n * 512:(n + 1) * 512]
                                     .rearrange("a (p c) n -> p a c n", p=P)).then_inc(w_loaded[4 + n], 16)

            load_unit(0)
            for t in range(TT):
                sp.dma_start(x_tok[:, t, :], x[0, t * P:(t + 1) * P, :]).then_inc(x_loaded[t], 16)
            load_unit(1)
            for dst, src in ((ws_nat[:, :, :], gmlp_w_s[0].rearrange("g i j -> i g j")),
                             (ln_g[:, :], gmlp_ln_g[0].partition_broadcast(P)),
                             (ln_b[:, :], gmlp_ln_b[0].partition_broadcast(P)),
                             (gate_bs[:, :, :], gmlp_b_s[0].partition_broadcast(P))):
                sp.dma_start(dst, src).then_inc(consts_loaded, 16)
            for c in range(2, UNITS - 2):
                load_unit(c)
                if c == GB + 3:
                    sp.wait_ge(att_ready, STEPS // 2)
                    sp.dma_start(h_tok[:, :, :], x[0].rearrange("(t p) d -> p t d", p=P)).then_inc(x_reloaded, 16)
            wait_unit_used(sp, WO - 2)
            load_experts(0, w_gate, 0, 1)
            load_unit(UNITS - 2)
            wait_unit_used(sp, WO - 1)
            sp.wait_ge(merged_ready, KT)
            load_experts(2, w_up, 0, 1)
            load_unit(UNITS - 1)
            load_down(0, 1)
            sp.wait_ge(dve_tile_done, 24)
            sp.dma_start(W[6][:, :], w_gate[0, 2].rearrange("(p c) n -> p (c n)", p=P)).then_inc(w_loaded[6], 16)
            sp.wait_ge(logitsT_done, 2)
            sp.dma_start(W[7][:, :], w_gate[0, 3].rearrange("(p c) n -> p (c n)", p=P)).then_inc(w_loaded[7], 16)

            sp.wait_ge(part2_ready, TT)
            sp.dma_start(W[8][:, :], w_up[0, 2].rearrange("(p c) n -> p (c n)", p=P)).then_inc(w_loaded[8], 16)
            for half, used in enumerate((gate_half_done, gate_done)):
                sp.wait_ge(used, 1)
                for s in range(2):
                    sp.dma_start(W[s][:, half * 4 * DE:(half + 1) * 4 * DE].rearrange("p (c n) -> p c n", n=DE),
                                 w_gate[0, 4 + s].rearrange("(p c) n -> p c n", p=P)[:, 4 * half:4 * half + 4, :]
                                 ).then_inc(w_loaded[s], 16)
            sp.wait_ge(up_done, 1)
            sp.dma_start(W[3][:, :], w_up[0, 3].rearrange("(p c) n -> p (c n)", p=P)).then_inc(w_loaded[3], 16)
            load_down(2, 3, used=1)

            def load_gate(i, even):
                sp.wait_ge(gate_done, i + 1)
                load_experts(0 if even else 6, w_gate, 2 * i + 4, 2 * i + 5)

            def load_up_down(i):
                sp.wait_ge(up_done, i + 1)
                load_experts(2, w_up, 2 * i + 2, 2 * i + 3)
                load_down(2 * i + 2, 2 * i + 3, used=i + 1)

            load_gate(1, False)
            load_up_down(1)
            with sp.Fori(1, FAR_PAIRS // 2) as j:
                for half in range(2):
                    load_gate(2 * j + half, half == 0)
                    load_up_down(2 * j + half)
            with sp.Fori(FAR_PAIRS // 2, PAIRS // 2 - 1) as j:
                for half in range(2):
                    load_up_down(2 * j + half)
                    load_gate(2 * j + half, half == 0)
            load_up_down(PAIRS - 2)
            sp.wait_ge(routed, 1)
            sp.dma_start(final_g[:, :], norm_final_g.partition_broadcast(P)).then_inc(late_loaded, 16)
            n_over = sp.value_load(ov_count[0:1, 0:1], min_val=0, max_val=OV_TILES)

            def overflow_loads(k, i, even):
                e0 = sp.value_load(ov_expert[0:1, bass.ds(2 * k, 1)], min_val=0, max_val=NE - 1)
                e1 = sp.value_load(ov_expert[0:1, bass.ds(2 * k + 1, 1)], min_val=0, max_val=NE - 1)
                sp.wait_ge(gate_done, i)
                load_experts(0 if even else 6, w_gate, e0, e1)
                sp.wait_ge(up_done, i)
                load_experts(2, w_up, e0, e1)
                load_down(e0, e1, used=i)

            with sp.If(n_over > 0):
                with sp.Fori(0, OV_PAIRS // 2) as j:
                    overflow_loads(2 * j, 2 * j + PAIRS, True)
                    overflow_loads(2 * j + 1, 2 * j + 1 + PAIRS, False)
            for t in (0, 2, 1, 3):
                sp.wait_ge(result_low if t < 2 else result_high, t % 2 + 1)
                sp.dma_start(out[0, t * P:(t + 1) * P, :], result[:, t, :]).then_inc(out_stored, 16)
            sp.wait_ge(out_stored, 16 * TT)

        @block.gpsimd
        def _(pool):
            pool.memset(ident[:, :], 0.0).then_inc(ident_made, 1)
            pool.wait_ge(ident_made, 1)
            pool.affine_select(out=ident[:, :], in_=ident[:, :], compare_op=ALU.not_equal, fill=1.0, base=0,
                               pattern=[[-1, P]], channel_multiplier=1).then_inc(ident_made, 1)
            pool.iota(dist_i[:, :], pattern=[[-1, BAND]], base=HD, channel_multiplier=1).then_inc(iota_made, 1)
            pool.wait_ge(att_ready, STEPS // 2)
            pool.wait_ge(merged_ready, KT)
            pool.memset(w_router[:, :, :], 0.0).then_inc(router_cleared, 1)
            pool.iota(row_iota[:, :], pattern=[[1, P]], base=0, channel_multiplier=0,
                      allow_small_or_imprecise_dtypes=True).then_inc(route_iotas_made, 1)
            pool.iota(expert_iota[:, :], pattern=[[1, NE]], base=0, channel_multiplier=0,
                      allow_small_or_imprecise_dtypes=True).then_inc(route_iotas_made, 1)
            pool.iota(first_row[:, :], pattern=[[ROWS, NE]], base=0, channel_multiplier=0,
                      allow_small_or_imprecise_dtypes=True).then_inc(route_iotas_made, 1)
            pool.iota(ov_iota[:, :], pattern=[[1, OV_TILES]], base=0, channel_multiplier=0,
                      allow_small_or_imprecise_dtypes=True).then_inc(route_iotas_made, 1)
            pool.iota(tile_ends[:, :, :], pattern=[[0, NE], [ROWS, MAX_OV]], base=ROWS, channel_multiplier=0,
                      allow_small_or_imprecise_dtypes=True).then_inc(route_iotas_made, 1)
            pool.memset(all_ones[:, :], 1.0).then_inc(route_iotas_made, 1)
            pool.wait_ge(route_iotas_made, 6)
            pool.affine_select(out=earlier[:, :], in_=all_ones[:, :], compare_op=ALU.is_gt, fill=0.0, base=0,
                               pattern=[[1, P]], channel_multiplier=-1).then_inc(route_iotas_made, 1)
            def first_rest(t):
                pool.wait_ge(part0_ready, t + 1)
                pool.tensor_tensor(hn_rest[:, t, :, :], hn_rest[:, t, :, :], hn_part[0][:, t, :, :],
                                   ALU.subtract).then_inc(rest_ready, 1)

            def third_part(t):
                pool.wait_ge(rest_ready, min(t + 2, TT))
                pool.wait_ge(part1_ready, t + 1)
                pool.tensor_tensor(hn_part[2][:, t, :, :], hn_rest[:, t, :, :], hn_part[1][:, t, :, :],
                                   ALU.subtract).then_inc(part2_ready, 1)

            first_rest(0)
            for t in range(1, TT):
                first_rest(t)
                third_part(t - 1)
            third_part(TT - 1)
            pool.wait_ge(late_loaded, 16 * 6)
            pool.wait_ge(h_final, 1)
            for t in range(2, TT):
                pool.tensor_tensor(result[:, t, :], h_tok[:, t, :], final_g[:, :], ALU.mult).then_inc(final_gained, 1)

        @block.tensor
        def _(pe):
            pe.wait_ge(ident_made, 2)
            pe.wait_ge(vecs_loaded, 16 * 3)
            pe.transpose(bank[7][:, 0:3 * KT], vec_rows[:, :], ident[0:3 * KT, 0:3 * KT]).then_inc(vecs_psum, 1)
            pe.wait_ge(normed_low, 2)
            for k in range(KT):
                if k == KT - 1:
                    pe.wait_ge(vecs_ready, 1)
                for t in range(2):
                    pe.transpose(bank[k][:, t * P:(t + 1) * P], xn_tok[:, t, k * P:(k + 1) * P], ident[:, :])
            pe.wait_ge(normed_high, 2)
            for k in range(KT):
                for t in range(2, TT):
                    mm = pe.transpose(bank[k][:, t * P:(t + 1) * P], xn_tok[:, t, k * P:(k + 1) * P], ident[:, :])
                mm.then_inc(xnT_psum, 1)

            def three(dst, hi_w, lo_w, hi_x, lo_x, start, stop):
                pe.matmul(dst, hi_w, hi_x, start=start, stop=False)
                pe.matmul(dst, hi_w, lo_x, start=False, stop=False)
                return pe.matmul(dst, lo_w, hi_x, start=False, stop=stop)

            def wide_unit(c, kh, xT_hi, xT_lo, done, before_last=None):
                pe.wait_ge(lo_split, c + 1)
                w_h = whi[c % 2][:, :].rearrange("p (k n) -> p k n", k=WIDE)
                w_l = wlo[c % 2][:, :].rearrange("p (k n) -> p k n", k=WIDE)
                for t in range(TT):
                    if before_last and t == TT - 1:
                        before_last()
                    if c < Q and kh == 0 and c >= 2:
                        pe.wait_ge(act_tile_read, 2 * c - 3 + t)
                    if c >= WO and kh == 0 and c >= WO + 2:
                        pe.wait_ge(h_ready, 2 * (c - WO) - 3 + t)
                    for k in range(WIDE):
                        kk = kh * WIDE + k
                        if c == WO and t == TT - 1 and k == 0:
                            pe.wait_ge(gate_used, 24)
                        if c == WO + 1 and t == k == 0:
                            pe.wait_ge(merged_ready, KT)
                        if c <= 1 and t == 0:
                            pe.wait_ge(xnT_ready, kk + 1)
                        ts = slice(t * P, (t + 1) * P)
                        dst = bank[t][:, :]
                        first, last = (kh == 0 and k == 0), (kh == 1 and k == WIDE - 1)
                        pe.matmul(dst, xT_hi[:, kk, ts], w_h[:, k, :], start=first, stop=False)
                        pe.matmul(dst, xT_hi[:, kk, ts], w_l[:, k, :], start=False, stop=False)
                        mm = pe.matmul(dst, xT_lo[:, kk, ts], w_h[:, k, :], start=False, stop=last)
                    if kh == 1:
                        mm.then_inc(done, 1)
                if kh == 0:
                    mm.then_inc(half_used, 1)

            def tall_tile(c, m, dst, xT_hi, xT_lo, done):
                if m == 0:
                    pe.wait_ge(lo_split, c + 1)
                w_h = whi[c % 2][:, :].rearrange("p (k n) -> p k n", k=TALL)
                w_l = wlo[c % 2][:, :].rearrange("p (k n) -> p k n", k=TALL)
                ms = slice(m * P, (m + 1) * P)
                for k in range(KT):
                    mm = three(dst, w_h[:, k, ms], w_l[:, k, ms], xT_hi[:, k, :], xT_lo[:, k, :],
                               k == 0, k == KT - 1)
                mm.then_inc(done, 1)

            def act_tile(c, m, a):
                pe.wait_ge(act_tile_read, a - 1)
                tall_tile(c, m, bank[a % 2][:, :], xnT_hi, xnT_lo, act_tile_done)

            def attention_slot(s):
                if s < STEPS:
                    pair, b, side = step_of(s)
                    if s == 0:
                        pe.wait_ge(act_tile_read, 20)
                    pe.wait_ge(scores_read, s)
                    ps = slice(side * HD, (side + 1) * HD)
                    lo = 0 if b else HD
                    for r in range(REP):
                        mm = pe.matmul(bank[3 + r // 2][:, (r % 2) * BAND + lo:(r % 2 + 1) * BAND],
                                       qT[ps, pair * REP + r, b * P:(b + 1) * P],
                                       kT[ps, pair, b * P - HD + lo:(b + 1) * P], start=True, stop=True)
                    mm.then_inc(scores_done, 1)
                if s >= 4 and s % 2 == 0:
                    n = s - 3
                    pair, b, _ = step_of(n)
                    pe.wait_ge(probsT_ready, n + 1)
                    pe.wait_ge(va_ready, 1)
                    pe.wait_ge(att_ready, n // 2)
                    for own in (True, False) if b else (True,):
                        for side in range(2):
                            kv = 2 * pair + side
                            dst = bank[7][side * HD:(side + 1) * HD, :]
                            if own:
                                mm = pe.matmul(dst, va_tok[:, b, kv * HD:(kv + 1) * HD],
                                               probsT[side][:, 0:REP * P], start=True, stop=(b == 0))
                            else:
                                mm = pe.matmul(dst.rearrange("p (r q) -> p r q", q=P)[:, :, 0:HD],
                                               va_tok[:, b - 1, kv * HD:(kv + 1) * HD],
                                               probsT[side][:, REP * P:].rearrange("p (r q) -> p r q", q=HD),
                                               start=False, stop=True)
                    mm.then_inc(pv_done, 1)
                if 2 <= s < STEPS + 2:
                    n = s - 2
                    _, b, _ = step_of(n)
                    pe.wait_ge(probs_ready, n + 1)
                    pe.wait_ge(probsT_ready, n)
                    for r in range(REP):
                        mm = pe.transpose(bank[5][:, r * P:(r + 1) * P], probs[n % 2][:, r, P:2 * P], ident[:, :])
                    for r in range(REP if b else 0):
                        mm = pe.transpose(bank[6][:, r * HD:(r + 1) * HD], probs[n % 2][0:HD, r, 0:P],
                                          ident[0:HD, 0:HD])
                    mm.then_inc(turned, 1)

            for c in range(ZV, Q):
                wide_unit(c, c % 2, xnT_hi, xnT_lo, act_tile_done)
                if c == 1:
                    pe.wait_ge(consts_loaded, 16 * 4)
                    for g in range(GROUPS):
                        mm = pe.transpose(bank[6 + g // 4][:, (g % 4) * P:(g % 4 + 1) * P], ws_nat[:, g, :], ident[:, :])
                    mm.then_inc(wsT_psum, 1)
            for c in range(Q, ZU):
                for m in range(2):
                    act_tile(c, m, 8 + 2 * (c - Q) + m)
            for c in range(ZU, GA):
                for m in range(2):
                    g = 2 * (c - ZU) + m
                    act_tile(c, m, 20 + g)
                    if g == 0:
                        pe.wait_ge(wsT_ready, 1)
                        pe.wait_ge(act_tile_read, 20)
                        for j in range(2):
                            for t in range(TT):
                                mm = pe.transpose(bank[6 + j][:, t * P:(t + 1) * P], vaT[:, j, t * P:(t + 1) * P], ident[:, :])
                        mm.then_inc(va_psum, 1)
                    pe.wait_ge(ln_ready, TT)
                    pe.wait_ge(gate_used, g)
                    for b in range(TT):
                        mm = pe.matmul(bank[2][:, b * P:(b + 1) * P], v_tok[:, b, g * P:(g + 1) * P], wsT[:, g, :],
                                       start=True, stop=True)
                    mm.then_inc(sv_done, 1)
                    if g >= 5:
                        attention_slot(g - 5)
            for u in range(4):
                for m in range(2):
                    act_tile(GA + 2 * u, m, 28 + 2 * u + m)
                    attention_slot(3 + 4 * u + m)
                for m in range(2):
                    if u == 0 and m == 0:
                        pe.wait_ge(sp_ready, KT)
                    d = 2 * u + m
                    pe.wait_ge(gate_used, 8 + d)
                    tall_tile(GA + 2 * u + 1, m, bank[2][:, :], spT_hi, spT_lo, dve_tile_done)
                    attention_slot(5 + 4 * u + m)
            for u in range(4):
                for m in range(2):
                    act_tile(GB + 2 * u, m, 36 + 2 * u + m)
                for m in range(2):
                    if u == 0 and m == 0:
                        pe.wait_ge(att_ready, STEPS // 2)
                    d = 8 + 2 * u + m
                    pe.wait_ge(gate_used, 8 + d - 1)
                    tall_tile(GB + 2 * u + 1, m, bank[2 + d % 2][:, :], attT_hi, attT_lo, dve_tile_done)
            pe.wait_ge(act_tile_read, 44)
            pe.wait_ge(merged_ready, KT - 1)
            def turn_h(t):
                pe.wait_ge(hg_ready, TT + t + 1)
                if t >= 2:
                    pe.wait_ge(hgT_a, t - 1)
                    pe.wait_ge(hgT_b, t - 1)
                for c in range(KT):
                    mm = pe.transpose(bank[4 + 2 * (t % 2) + c // 4][:, (c % 4) * P:(c % 4 + 1) * P],
                                      hg[:, t, c, :], ident[:, :])
                mm.then_inc(hgT_psum, 1)

            def route(j):
                pe.wait_ge(hgT_a, 2 * j + 2)
                pe.wait_ge(hgT_b, 2 * j + 2)
                pe.wait_ge(h_ready, TT + 1 + j)
                if j == 0:
                    pe.wait_ge(late_loaded, 16 * 5)
                for c in range(KT):
                    mm = pe.matmul(bank[j][(c % 2) * 64:(c % 2 + 1) * 64, 0:2 * P], w_router[:, c, :], hgT[j][:, c, :],
                                   start=(c < 2), stop=(c >= KT - 2))
                mm.then_inc(logitsT_done, 1)

            def turn_first_tiles():
                for t in range(2):
                    turn_h(t)

            for c in range(WO, UNITS):
                wide_unit(c, c % 2, mgT_hi, mgT_lo, dve_tile_done, turn_first_tiles if c == UNITS - 1 else None)
            route(0)
            turn_h(2)
            turn_h(3)
            route(1)
            pe.wait_ge(h_ready, 8)
            for t in range(TT):
                pe.wait_ge(logitsT_ready, t // 2 + 1)
                mm = pe.transpose(bank[2][:, t * P:(t + 1) * P], logitsT[:, t * P:(t + 1) * P], ident[:, :])
            mm.then_inc(logits_turned, 1)
            pe.wait_ge(picked_ready, 1)
            pe.wait_ge(route_iotas_made, 7)
            for t in range(TT):
                for tp in range(t + 1):
                    mm = pe.matmul(bank[3][:, t * NE:(t + 1) * NE], earlier[:, :] if tp == t else all_ones[:, :],
                                   picked[:, tp, :], start=(tp == 0), stop=(tp == t))
            for t in range(TT):
                mm = pe.matmul(bank[0][:, 0:NE], all_ones[:, :], picked[:, t, :], start=(t == 0), stop=(t == TT - 1))
            mm.then_inc(ranks_done, 1)

            def gather_rows(i, tiles):
                for c in tiles:
                    if c == 0:
                        pe.wait_ge(onehot_ready, i + 1)
                    for t in range(TT):
                        for j in range(3):
                            mm = pe.matmul(bank[2 + c // 4][:, (c % 4) * P:(c % 4 + 1) * P],
                                           hn_part[j][:, t, c, :], onehot[:, t, :],
                                           start=(t == 0 and j == 0), stop=(t == TT - 1 and j == 2))
                    if c % 4 == 3:
                        mm.then_inc(pack_done, 1)

            def project(buffers, dst, done, packed=None, half_done=None):
                for u, loaded in buffers:
                    pe.wait_ge(w_loaded[u], loaded)
                for c in range(KT):
                    if packed is not None and c == 0:
                        pe.wait_ge(pack_a, packed)
                    if packed is not None and c == 4:
                        pe.wait_ge(pack_b, packed)
                    for s, (u, _) in enumerate(buffers):
                        mm = pe.matmul(dst[s * ROWS:(s + 1) * ROWS, :], packT[:, c, s * ROWS:(s + 1) * ROWS],
                                       W[u][:, c * DE:(c + 1) * DE], start=(c == 0), stop=(c == KT - 1))
                    if half_done is not None and c == 3:
                        mm.then_inc(half_done, 1)
                mm.then_inc(done, 1)

            def expert_pair(i, gate, up, half_done=None):
                project(gate, bank[0], gate_done, packed=i + 1, half_done=half_done)
                for t in range(TT):
                    mm = pe.transpose(bank[7][:, t * P:(t + 1) * P], weight_a[:, t, :], ident[:, :])
                mm.then_inc(weights_turned, 1)
                project(up, bank[1], up_done)
                gather_rows(i + 1, (0, 1))
                pe.wait_ge(rows_ready, i + 1)
                for c in range(FT):
                    mm = pe.transpose(bank[4][:, c * P:(c + 1) * P], act_rows[:, c, :], ident[:, :])
                mm.then_inc(rows_turned, 1)
                gather_rows(i + 1, (2, 3))
                pe.wait_ge(actT_ready, i + 1)
                for n, done in enumerate((y_left, y_right)):
                    pe.wait_ge(w_loaded[4 + n], 32 * i + 32)
                    for c in range(FT):
                        for s in range(2):
                            mm = pe.matmul(bank[5 + n][s * ROWS:(s + 1) * ROWS, :], actT[:, c, s * ROWS:(s + 1) * ROWS],
                                           W[4 + s][:, c * D + n * 512:c * D + (n + 1) * 512],
                                           start=(c == 0), stop=(c == FT - 1))
                    mm.then_inc(done, 1)
                pe.wait_ge(onehotT_ready, i + 1)
                for n in range(2):
                    pe.wait_ge(y_lo_ready, 2 * i + n + 1)
                    for t in range(TT):
                        if n == 1 and t >= 2:
                            pe.wait_ge(h_added, 8 * i + t - 1)
                        dst = bank[SPREAD_BANKS[n][t]][:, :]
                        pe.matmul(dst, onehotT[:, t * P:(t + 1) * P], y_hi[:, n * 512:(n + 1) * 512], start=True, stop=False)
                        pe.matmul(dst, onehotT[:, t * P:(t + 1) * P], y_lo[:, n * 512:(n + 1) * 512],
                                  start=False, stop=True).then_inc(spread_done, 1)
                gather_rows(i + 1, (4, 5, 6, 7))
                pe.wait_ge(h_added, 8 * i + 8)

            pe.wait_ge(part2_ready, TT)
            pe.wait_ge(ranks_read, 1)
            gather_rows(0, range(KT))
            pe.wait_ge(counts_read, 1)

            def even_and_odd_pair(j):
                expert_pair(2 * j, gate=((0, 16 * j + 32), (1, 16 * j + 32)), up=((2, 32 * j), (3, 32 * j + 16)))
                expert_pair(2 * j + 1, gate=((6, 16 * j + 16), (7, 16 * j + 16)),
                            up=((2, 32 * j + 16), (3, 32 * j + 32)))

            expert_pair(0, gate=((0, 16), (1, 16)), up=((2, 16), (3, 16)), half_done=gate_half_done)
            expert_pair(1, gate=((6, 16), (7, 16)), up=((8, 16), (3, 32)))
            with pe.Fori(1, PAIRS // 2) as j:
                even_and_odd_pair(j)
            n_over = pe.value_load(ov_count[0:1, 0:1], min_val=0, max_val=OV_TILES)
            with pe.If(n_over > 0):
                with pe.Fori(PAIRS // 2, (PAIRS + OV_PAIRS) // 2) as j:
                    even_and_odd_pair(j)

        @block.scalar
        def _(act):
            consts = [(vec_rows[0:KT, :], norm_mix_g[0].rearrange("(k p) -> k p", p=P)),
                      (vec_rows[KT:3 * KT, :], gate_bias[0].rearrange("(k p) -> k p", p=P)),
                      (sinks, attn_sinks[0].partition_broadcast(P))]
            for dst, src in consts:
                act.dma_start(dst, src).then_inc(vecs_loaded, 16)
            def split_hi(c):
                act.wait_ge(unit_loaded[c % 2], landed[c])
                if c >= 2:
                    wait_unit_used(act, c - 2)
                act.activation(whi[c % 2][:, :], raw[c % 2][:, :], ACT.Copy).then_inc(hi_split, 1)

            def start_unit(c):
                if c + 1 < UNITS:
                    split_hi(c + 1)

            def gate_tile(a, func, **kw):
                act.wait_ge(act_tile_done, a + 1)
                if a - 20 >= 2:
                    act.wait_ge(gate_used, a - 20 - 1)
                act.activation(gbuf[a % 2][:, :], bank[a % 2][:, :], func, **kw).then_inc(act_tile_read, 1)

            def attention_slot(s):
                if 2 <= s < STEPS + 2:
                    n = s - 2
                    _, b, _ = step_of(n)
                    act.wait_ge(turned, n + 1)
                    if n >= 2:
                        act.wait_ge(pv_done, n // 2)
                    last = act.activation(probsT[n % 2][:, 0:512], bank[5][:, :], ACT.Copy)
                    if b:
                        last = act.activation(probsT[n % 2][:, 512:768], bank[6][:, 0:256], ACT.Copy)
                    last.then_inc(probsT_ready, 1)
                if s < STEPS:
                    _, b, _ = step_of(s)
                    lo = HD if b else P
                    act.wait_ge(negmax_ready, s + 1)
                    for r in range(REP):
                        row = probs[s % 2][:, r, lo:]
                        act.activation(row, row, ACT.Exp, bias=neg_max[s % 2][:, r:r + 1],
                                       accum_out=denom[s % 2][:, r:r + 1])
                    act.activation(sink_e[s % 2], sink_e[s % 2], ACT.Exp).then_inc(exp_done, 1)

            split_hi(0)
            for t in range(TT):
                act.wait_ge(x_loaded[t], 16)
                act.activation(xn_tok[:, t, :], x_tok[:, t, :], ACT.Square, scale=float(D) ** -0.5,
                               accum_out=mean_sq[:, t:t + 1]).then_inc(square_summed, 1)
            act.wait_ge(x_rstd_ready, 1)
            for t in range(2, TT):
                act.activation(xn_tok[:, t, :], x_tok[:, t, :], ACT.Copy, scale=rstd[:, t:t + 1]).then_inc(normed_high, 1)
            act.wait_ge(vecs_ready, 1)
            for k in range(KT):
                act.wait_ge(xnT_psum, k + 1)
                act.activation(xnT_hi[:, k, :], bank[k][:, :], ACT.Copy, scale=mix_g[:, k:k + 1]).then_inc(xhi_ready, 1)
            for c in range(ZV, Q):
                start_unit(c)
                for t in range(TT if c % 2 else 0):
                    a = 4 * (c // 2) + t
                    act.wait_ge(act_tile_done, a + 1)
                    act.activation(v_tok[:, t, (c // 2) * 512:(c // 2 + 1) * 512], bank[t][:, :],
                                   ACT.Gelu).then_inc(act_tile_read, 1)
            for c in range(Q, ZU):
                start_unit(c)
                for m in range(2):
                    j = 2 * (c - Q) + m
                    act.wait_ge(act_tile_done, 8 + j + 1)
                    if j == 0:
                        act.wait_ge(wsT_psum, 1)
                    dst = qT[:, j, :] if j < 8 else kT[:, j - 8, :] if j < 10 else vaT[:, j - 10, :]
                    act.activation(dst, bank[j % 2][:, :], ACT.Copy).then_inc(act_tile_read, 1)
            for c in range(ZU, GA):
                start_unit(c)
                for m in range(2):
                    g = 2 * (c - ZU) + m
                    gate_tile(20 + g, ACT.Gelu)
                    if g >= 5:
                        attention_slot(g - 5)
            for u in range(4):
                start_unit(GA + 2 * u)
                for m in range(2):
                    j = 2 * u + m
                    gate_tile(28 + j, ACT.Tanh, bias=gate_b[:, j:j + 1], scale=0.5)
                    attention_slot(3 + 4 * u + m)
                start_unit(GA + 2 * u + 1)
                for m in range(2):
                    attention_slot(5 + 4 * u + m)
            for u in range(4):
                start_unit(GB + 2 * u)
                for m in range(2):
                    j = 2 * u + m
                    gate_tile(36 + j, ACT.Tanh, bias=gate_b[:, KT + j:KT + j + 1], scale=0.5)
                start_unit(GB + 2 * u + 1)
            act.wait_ge(merged_ready, KT)
            late = [(ffn_g[:, :], norm_ffn_g[0].partition_broadcast(P)),
                    (w_router[:, :, 0:NG], w_router_group[0].rearrange("(p c) n -> p c n", p=P)),
                    (w_router[:, :, NG:NR], w_router_expert[0].rearrange("(p c) n -> p c n", p=P)),
                    (b_router[:, 0:NG], b_router_group[0].partition_broadcast(P)),
                    (b_router[:, NG:NR], b_router_expert[0].partition_broadcast(P))]
            act.wait_ge(router_cleared, 1)
            for dst, src in late:
                act.dma_start(dst, src).then_inc(late_loaded, 16)
            for c in range(WO, UNITS):
                start_unit(c)
            def square_h(n, t):
                act.wait_ge(h_ready, TT * n + t + 1)
                if n or t:
                    act.wait_ge(hsq_summed, TT * n + t)
                act.activation(squares[:, :], h_tok[:, t, n * 512:(n + 1) * 512], ACT.Square, scale=float(D) ** -0.5,
                               accum_out=half_sq[:, TT * n + t:TT * n + t + 1]).then_inc(hsq_summed, 1)

            def copy_hgT(t):
                act.wait_ge(hgT_psum, t + 1)
                act.activation(hgT[t // 2][:, 0:4, (t % 2) * P:(t % 2 + 1) * P],
                               bank[4 + 2 * (t % 2)][:, :].rearrange("p (c q) -> p c q", c=4), ACT.Copy).then_inc(hgT_a, 1)

            for t in range(TT):
                square_h(0, t)
            for t in range(TT - 1):
                square_h(1, t)
            def scale_h(t):
                act.wait_ge(rstd_ready, t // 2 + 1)
                act.activation(hn_rest[:, t, :, :], hg[:, t, :, :], ACT.Copy, scale=rstd[:, t:t + 1]).then_inc(hn_ready, 1)

            def first_part(t):
                act.wait_ge(hn_ready, t + 1)
                act.activation(hn_part[0][:, t, :, :], hn_rest[:, t, :, :], ACT.Copy).then_inc(part0_ready, 1)

            def second_part(t):
                act.wait_ge(rest_ready, t + 1)
                act.activation(hn_part[1][:, t, :, :], hn_rest[:, t, :, :], ACT.Copy).then_inc(part1_ready, 1)

            copy_hgT(0)
            copy_hgT(1)
            scale_h(0)
            first_part(0)
            square_h(1, TT - 1)
            scale_h(1)
            copy_hgT(2)
            copy_hgT(3)
            first_part(1)
            second_part(0)
            scale_h(2)
            first_part(2)
            act.wait_ge(route_sub, 1)
            act.activation(gexp[:, :, :], gexp[:, :, :], ACT.Exp).then_inc(route_exp, 1)
            second_part(1)
            scale_h(3)
            first_part(3)
            second_part(2)
            act.wait_ge(route_sub, 2)
            act.activation(r4[5], r4[5], ACT.Exp).then_inc(route_exp, 1)
            second_part(3)

            def copy_pack(i):
                act.wait_ge(pack_done, 2 * i + 1)
                act.activation(packT[:, 0:4, :], bank[2][:, :].rearrange("p (c q) -> p c q", c=4),
                               ACT.Copy).then_inc(pack_a, 1)

            def expert_pair(i):
                copy_pack(i)
                act.wait_ge(gate_done, i + 1)
                act.activation(silu_g[:, :], bank[0][:, :], ACT.Silu).then_inc(silu_ready, 1)
                act.wait_ge(rows_turned, i + 1)
                act.activation(actT[:, :, :], bank[4][:, :].rearrange("p (c q) -> p c q", c=FT),
                               ACT.Copy).then_inc(actT_ready, 1)
                act.wait_ge(row_weight_ready, i + 1)
                for n, done in enumerate((y_left, y_right)):
                    act.wait_ge(done, i + 1)
                    act.activation(y_hi[:, n * 512:(n + 1) * 512], bank[5 + n][:, :], ACT.Copy,
                                   scale=row_weight).then_inc(y_hi_ready, 1)

            act.wait_ge(h_ready, 8)
            with act.Fori(0, PAIRS) as i:
                expert_pair(i)
            n_over = act.value_load(ov_count[0:1, 0:1], min_val=0, max_val=OV_TILES)
            with act.If(n_over > 0):
                with act.Fori(PAIRS, PAIRS + OV_PAIRS) as i:
                    expert_pair(i)
            act.wait_ge(h_final, 1)
            for t in range(2):
                if t:
                    act.wait_ge(ysq_summed, t)
                act.activation(result[:, t, :], h_tok[:, t, :], ACT.Square, scale=float(D) ** -0.5,
                               accum_out=mean_sq[:, t:t + 1]).then_inc(ysq_summed, 1)
            act.wait_ge(y_rstd_ready, 1)
            for t in range(2, TT):
                act.wait_ge(final_gained, t - 1)
                act.activation(result[:, t, :], result[:, t, :], ACT.Copy, scale=rstd[:, t:t + 1]).then_inc(result_high, 1)

        @block.vector
        def _(dve):
            steps = [0]

            def then(instruction):
                instruction.then_inc(dve_step, 1)
                steps[0] += 1
                dve.wait_ge(dve_step, steps[0])

            def inverse_root(y, value):
                then(dve.tensor_scalar(value, value, EPS, None, ALU.add))
                then(dve.tensor_scalar(y.bitcast(I32), value.bitcast(I32), -0.5, float(0x5F3759DF), ALU.mult, ALU.add))
                for _ in range(3):
                    work = root_work[:, 0:y.shape[1]]
                    then(dve.tensor_tensor(work, y, value, ALU.mult))
                    then(dve.scalar_tensor_tensor(out=work, in0=work, scalar=-0.5, in1=y, op0=ALU.mult, op1=ALU.mult))
                    then(dve.scalar_tensor_tensor(out=y, in0=work, scalar=1.5, in1=y, op0=ALU.add, op1=ALU.mult))

            dve.memset(probs[0][:, :, 0:HD], 0.0)
            dve.memset(probs[1][:, :, 0:HD], 0.0)
            def split_lo(c):
                dve.wait_ge(hi_split, c + 1)
                dve.tensor_tensor(wlo[c % 2][:, :], raw[c % 2][:, :], whi[c % 2][:, :].bitcast(F32),
                                  ALU.subtract).then_inc(lo_split, 1)

            def start_unit(c):
                if c + 1 < UNITS:
                    split_lo(c + 1)

            def make_alibi():
                dve.wait_ge(iota_made, 1)
                then(dve.tensor_copy(dist[:, :], dist_i[:, :]))
                then(dve.scalar_tensor_tensor(out=dist[:, :], in0=dist[:, :], scalar=-1.0, in1=dist[:, :],
                                              op0=ALU.mult, op1=ALU.max))
                then(dve.memset(band_mask[:, :], 0.0))
                dve.memset(band_mask[0:HD, 2 * HD:BAND], MASKED)
                then(dve.memset(band_mask[HD:P, 0:HD], MASKED))
                for h in range(H):
                    last = dve.scalar_tensor_tensor(out=alibi[:, h, :], in0=dist[:, :], scalar=-slopes[h],
                                                    in1=band_mask[:, :], op0=ALU.mult, op1=ALU.add)
                last.then_inc(alibi_ready, 1)
                then(dve.tensor_scalar(gate_b, gate_b, 0.5, None, ALU.mult))

            def layernorm_stats():
                dve.wait_ge(consts_loaded, 16 * 4)
                for t in range(TT):
                    dve.wait_ge(act_tile_read, 4 + t + 1)
                    for n in range(2):
                        last = dve.bn_stats(ln_stats[:, t * 12 + n * 6:t * 12 + (n + 1) * 6],
                                            v_tok[:, t, n * 512:(n + 1) * 512])
                    then(last)
                    then(dve.bn_aggr(ln_mv[:, 2 * t:2 * t + 2], ln_stats[:, t * 12:(t + 1) * 12]))
                then(dve.tensor_copy(mean_sq, ln_mv.rearrange("p (t s) -> p t s", s=2)[:, :, 1]))
                inverse_root(rstd, mean_sq)

            def layernorm(t):
                row = v_tok[:, t, :]
                then(dve.tensor_scalar(row, row, ln_mv[:, 2 * t:2 * t + 1], rstd[:, t:t + 1], ALU.subtract, ALU.mult))
                then(dve.tensor_tensor(row, row, ln_g[:, :], ALU.mult))
                dve.tensor_tensor(row, row, ln_b[:, :], ALU.add).then_inc(ln_ready, 1)

            def attention_slot(s):
                if 1 <= s < STEPS + 1:
                    n = s - 1
                    _, b, _ = step_of(n)
                    lo = HD if b else P
                    dve.wait_ge(exp_done, n + 1)
                    then(dve.tensor_tensor(denom[n % 2], denom[n % 2], sink_e[n % 2], ALU.add))
                    then(dve.reciprocal(denom[n % 2], denom[n % 2]))
                    p = probs[n % 2][:, :, lo:]
                    dve.tensor_tensor(p, p, denom[n % 2].unsqueeze(2).to_broadcast([P, REP, 2 * P - lo]),
                                      ALU.mult).then_inc(probs_ready, 1)
                if s < STEPS:
                    pair, b, side = step_of(s)
                    kv = 2 * pair + side
                    skip = 0 if b else HD
                    if s == 0:
                        dve.wait_ge(alibi_ready, 1)
                    dve.wait_ge(scores_done, s + 1)
                    if s >= 2:
                        dve.wait_ge(turned, s - 1)
                    for r in range(0, REP, 2):
                        last = dve.scalar_tensor_tensor(
                            out=probs[s % 2][:, r:r + 2, HD + skip:],
                            in0=bank[3 + r // 2][:, 0:2 * BAND].rearrange("p (r k) -> p r k", r=2)[:, :, skip:],
                            scalar=SCALE, in1=alibi[:, REP * kv + r:REP * kv + r + 2, skip:], op0=ALU.mult, op1=ALU.add)
                    last.then_inc(scores_read, 1)
                    dve.wait_ge(scores_read, s + 1)
                    sink = sinks[:, REP * kv:REP * (kv + 1)]
                    then(dve.tensor_reduce(neg_max[s % 2], probs[s % 2][:, :, HD + skip:], AX.X, ALU.max))
                    then(dve.tensor_tensor(neg_max[s % 2], neg_max[s % 2], sink, ALU.max))
                    then(dve.tensor_scalar(neg_max[s % 2], neg_max[s % 2], -1.0, None, ALU.mult))
                    dve.tensor_tensor(sink_e[s % 2], sink, neg_max[s % 2], ALU.add).then_inc(negmax_ready, 1)
                if s >= 4 and s % 2 == 0:
                    n = s - 3
                    pair, b, _ = step_of(n)
                    dve.wait_ge(pv_done, n // 2 + 1)
                    src = bank[7][:, :].rearrange("p (r q) -> p r q", q=P)
                    hi = attT_hi[:, pair * REP:(pair + 1) * REP, b * P:(b + 1) * P]
                    lo = attT_lo[:, pair * REP:(pair + 1) * REP, b * P:(b + 1) * P]
                    then(dve.tensor_copy(hi, src))
                    dve.tensor_tensor(lo, src, hi.bitcast(F32), ALU.subtract).then_inc(att_ready, 1)

            split_lo(0)
            dve.wait_ge(vecs_loaded, 16 * 3)
            dve.wait_ge(vecs_psum, 1)
            dve.tensor_copy(small[:, 0:3 * KT], bank[7][:, 0:3 * KT]).then_inc(vecs_ready, 1)
            dve.wait_ge(vecs_ready, 1)
            dve.wait_ge(square_summed, TT)
            inverse_root(rstd, mean_sq)
            dve.memset(root_work, 0.0).then_inc(x_rstd_ready, 1)
            for t in range(2):
                dve.tensor_scalar(xn_tok[:, t, :], x_tok[:, t, :], rstd[:, t:t + 1], None, ALU.mult).then_inc(normed_low, 1)
            for k in range(KT):
                dve.wait_ge(xhi_ready, k + 1)
                dve.scalar_tensor_tensor(out=xnT_lo[:, k, :], in0=bank[k][:, :], scalar=mix_g[:, k:k + 1],
                                         in1=xnT_hi[:, k, :].bitcast(F32), op0=ALU.mult,
                                         op1=ALU.subtract).then_inc(xnT_ready, 1)
            for c in range(ZV, Q):
                start_unit(c)
                if c == 0:
                    make_alibi()
                if c == 1:
                    dve.wait_ge(wsT_psum, 1)
                    for g4 in range(2):
                        last = dve.tensor_copy(wsT[:, 4 * g4:4 * g4 + 4, :],
                                               bank[6 + g4][:, :].rearrange("p (g i) -> p g i", g=4))
                    then(last)
                    dve.memset(wsT[HD:P, :, 0:HD], 0.0).then_inc(wsT_ready, 1)
            for c in range(Q, ZU):
                start_unit(c)
                if c == Q:
                    layernorm_stats()
                if c - Q < TT:
                    layernorm(c - Q)
            for c in range(ZU, GA):
                for m in range(2):
                    g = 2 * (c - ZU) + m
                    if m == 1:
                        start_unit(c)
                    if g == 0:
                        dve.wait_ge(va_psum, 1)
                        for j in range(2):
                            last = dve.tensor_copy(va_tok[:, :, j * P:(j + 1) * P],
                                                   bank[6 + j][:, :].rearrange("p (t c) -> p t c", t=TT))
                        last.then_inc(va_ready, 1)
                    dve.wait_ge(sv_done, g + 1)
                    dve.wait_ge(act_tile_read, 20 + g + 1)
                    dve.wait_ge(sp_ready, g)
                    then(dve.tensor_tensor(gated[:, :].rearrange("p (b i) -> p b i", b=TT),
                                           bank[2][:, :].rearrange("p (b i) -> p b i", b=TT),
                                           gate_bs[:, g:g + 1, :].to_broadcast([P, TT, P]), ALU.add))
                    dve.tensor_tensor(gated[:, :], gbuf[g % 2][:, :], gated[:, :], ALU.mult).then_inc(gate_used, 1)
                    dve.wait_ge(gate_used, g + 1)
                    then(dve.tensor_copy(spT_hi[:, g, :], gated[:, :]))
                    dve.tensor_tensor(spT_lo[:, g, :], gated[:, :], spT_hi[:, g, :].bitcast(F32),
                                      ALU.subtract).then_inc(sp_ready, 1)
                    if g >= 5:
                        attention_slot(g - 5)
            for u in range(4):
                for m in range(2):
                    attention_slot(3 + 4 * u + m)
                    if m == 0:
                        start_unit(GA + 2 * u)
                for m in range(2):
                    d = 2 * u + m
                    dve.wait_ge(dve_tile_done, d + 1)
                    dve.wait_ge(act_tile_read, 28 + d + 1)
                    dve.scalar_tensor_tensor(out=branch_a[:, d, :], in0=gbuf[d % 2][:, :], scalar=1.0, in1=bank[2][:, :],
                                             op0=ALU.add, op1=ALU.mult).then_inc(gate_used, 1)
                    attention_slot(5 + 4 * u + m)
                    if m == 0:
                        start_unit(GA + 2 * u + 1)
            for u in range(4):
                start_unit(GB + 2 * u)
                start_unit(GB + 2 * u + 1)
                for m in range(2):
                    j = 2 * u + m
                    dve.wait_ge(dve_tile_done, 8 + j + 1)
                    dve.wait_ge(act_tile_read, 36 + j + 1)
                    dve.wait_ge(merged_ready, j)
                    dve.scalar_tensor_tensor(out=merged[:, :], in0=gbuf[j % 2][:, :], scalar=1.0, in1=bank[2 + j % 2][:, :],
                                             op0=ALU.add, op1=ALU.mult).then_inc(gate_used, 1)
                    dve.wait_ge(gate_used, 16 + j + 1)
                    then(dve.tensor_tensor(merged[:, :], merged[:, :], branch_a[:, j, :], ALU.add))
                    then(dve.tensor_scalar(mgT_hi[:, j, :], merged[:, :], 0.5, None, ALU.mult))
                    dve.scalar_tensor_tensor(out=mgT_lo[:, j, :], in0=merged[:, :], scalar=0.5,
                                             in1=mgT_hi[:, j, :].bitcast(F32), op0=ALU.mult,
                                             op1=ALU.subtract).then_inc(merged_ready, 1)
            def add_h(n, t):
                dve.wait_ge(dve_tile_done, 16 + 4 * n + t + 1)
                part = h_tok[:, t, n * 512:(n + 1) * 512]
                dve.tensor_tensor(part, bank[t][:, :], part, ALU.add).then_inc(h_ready, 1)

            def gain_h(n, t):
                half = slice(n * 512, (n + 1) * 512)
                dve.wait_ge(h_ready, TT * n + t + 1)
                dve.tensor_tensor(hg[:, t, :, n * 64:(n + 1) * 64].rearrange("q c p -> q p c"),
                                  h_tok[:, t, half].rearrange("q (p c) -> q p c", c=KT),
                                  ffn_g[:, half].rearrange("q (p c) -> q p c", c=KT), ALU.mult).then_inc(hg_ready, 1)

            def copy_hgT(t):
                dve.wait_ge(hgT_psum, t + 1)
                dve.tensor_copy(hgT[t // 2][:, 4:8, (t % 2) * P:(t % 2 + 1) * P],
                                bank[5 + 2 * (t % 2)][:, :].rearrange("p (c q) -> p c q", c=4)).then_inc(hgT_b, 1)

            def copy_logitsT(j):
                dve.wait_ge(logitsT_done, j + 1)
                dve.tensor_copy(logitsT[:, j * 2 * P:(j + 1) * 2 * P], bank[j][:, 0:2 * P]).then_inc(logitsT_ready, 1)

            start_unit(WO)
            start_unit(WO + 1)
            dve.wait_ge(x_reloaded, 16)
            for t in range(TT):
                add_h(0, t)
            start_unit(WO + 2)
            dve.wait_ge(lo_split, UNITS)
            dve.wait_ge(late_loaded, 16 * 5)
            for t in range(TT):
                gain_h(0, t)
            def norm_h(pair):
                part = slice(2 * pair, 2 * pair + 2)
                dve.wait_ge(hsq_summed, TT + 2 * pair + 2)
                then(dve.tensor_tensor(mean_sq[:, part], half_sq[:, part],
                                       half_sq[:, TT + 2 * pair:TT + 2 * pair + 2], ALU.add))
                inverse_root(rstd[:, part], mean_sq[:, part])
                dve.memset(root_work, 0.0).then_inc(rstd_ready, 1)

            for t in range(TT):
                if t == 2:
                    norm_h(0)
                if t == TT - 1:
                    copy_hgT(0)
                    copy_hgT(1)
                add_h(1, t)
                gain_h(1, t)
            copy_logitsT(0)
            copy_hgT(2)
            copy_hgT(3)
            norm_h(1)
            copy_logitsT(1)

            def wide_t(a, n):
                return a.unsqueeze(2).to_broadcast([P, TT, n])

            def wide_e(a, n=NE):
                return a[:, 0:n].unsqueeze(1).to_broadcast([P, TT, n])

            dve.wait_ge(logits_turned, 1)
            two_parts = bank[2][:, :].rearrange("p (t s n) -> p t s n", t=TT, s=2)
            then(dve.tensor_copy(logits[:, :, :], two_parts[:, :, 0, 0:NR]))
            then(dve.tensor_tensor(logits[:, :, :], logits[:, :, :], two_parts[:, :, 1, 0:NR], ALU.add))
            then(dve.tensor_tensor(logits[:, :, :], logits[:, :, :], wide_t(rstd, NR), ALU.mult))
            then(dve.tensor_tensor(logits[:, :, :], logits[:, :, :], wide_e(b_router, NR), ALU.add))
            dve.wait_ge(route_iotas_made, 7)
            glog, elog = logits[:, :, 0:NG], logits[:, :, NG:NR]
            gmax, best, p_group, v1, v2, gap = r4[:6]

            def first_of(values, top, chosen, work, n):
                then(dve.tensor_tensor(work, values, wide_t(top, n), ALU.is_equal))
                then(dve.scalar_tensor_tensor(out=work, in0=work, scalar=-64.0, in1=wide_e(expert_iota, n),
                                              op0=ALU.mult, op1=ALU.add))
                then(dve.tensor_reduce(best, work, AX.X, ALU.min))
                then(dve.tensor_tensor(chosen, work, wide_t(best, n), ALU.is_equal))

            then(dve.tensor_reduce(gmax, glog, AX.X, ALU.max))
            dve.tensor_tensor(gexp[:, :, :], glog, wide_t(gmax, NG), ALU.subtract).then_inc(route_sub, 1)
            first_of(glog, gmax, gsel[:, :, :], gcand[:, :, :], NG)
            then(dve.tensor_scalar(gcand[:, :, :], gsel[:, :, :], -1.0, -MASKED, ALU.add, ALU.mult))
            then(dve.tensor_tensor(em[:, :, :].rearrange("p t (g e) -> p t g e", g=NG),
                                   elog.rearrange("p t (g e) -> p t g e", g=NG),
                                   gcand[:, :, :].unsqueeze(3).to_broadcast([P, TT, NG, EPG]), ALU.add))
            then(dve.tensor_reduce(v1, em[:, :, :], AX.X, ALU.max))
            first_of(em[:, :, :], v1, sel_a[:, :, :], cand[:, :, :], NE)
            then(dve.scalar_tensor_tensor(out=em[:, :, :], in0=sel_a[:, :, :], scalar=2 * MASKED, in1=em[:, :, :],
                                          op0=ALU.mult, op1=ALU.add))
            then(dve.tensor_reduce(v2, em[:, :, :], AX.X, ALU.max))
            dve.tensor_tensor(gap, v2, v1, ALU.subtract).then_inc(route_sub, 1)
            first_of(em[:, :, :], v2, sel_b[:, :, :], cand[:, :, :], NE)
            dve.tensor_tensor(picked[:, :, :], sel_a[:, :, :], sel_b[:, :, :], ALU.add).then_inc(picked_ready, 1)
            dve.wait_ge(route_exp, 2)
            dve.tensor_scalar(v1, gap, 1.0, None, ALU.add)
            then(dve.tensor_reduce(p_group, gexp[:, :, :], AX.X, ALU.add))
            then(dve.tensor_tensor(v1, v1, p_group, ALU.mult))
            then(dve.reciprocal(w_first, v1))
            dve.tensor_tensor(w_second, gap, w_first, ALU.mult)
            dve.wait_ge(ranks_done, 1)
            ranks = bank[3][:, 0:TT * NE].rearrange("p (t e) -> p t e", t=TT)
            dve.tensor_scalar(beyond[:, :, :], ranks, float(ROWS), None, ALU.is_ge)
            then(dve.tensor_tensor(rank[:, :, :], ranks, wide_e(first_row), ALU.add))
            dve.scalar_tensor_tensor(out=rank[:, :, :], in0=beyond[:, :, :], scalar=FAR, in1=rank[:, :, :],
                                     op0=ALU.mult, op1=ALU.add).then_inc(ranks_read, 1)
            dve.wait_ge(ranks_read, 1)
            for chosen, rows in ((sel_a, row_first), (sel_b, row_second)):
                then(dve.tensor_tensor(cand[:, :, :], chosen[:, :, :], rank[:, :, :], ALU.mult))
                then(dve.tensor_reduce(rows, cand[:, :, :], AX.X, ALU.add))

            def make_onehot(i):
                for t in range(TT):
                    for weights, row, w in ((weight_a, row_first, w_first), (weight_b, row_second, w_second)):
                        dve.tensor_scalar(weights[:, t, :], row_iota[:, :], row[:, t:t + 1], w[:, t:t + 1],
                                          ALU.is_equal, ALU.mult).then_inc(row_step, 1)
                dve.wait_ge(row_step, 10 * i + 8)
                dve.tensor_tensor(weight_a[:, :, :], weight_a[:, :, :], weight_b[:, :, :], ALU.add).then_inc(row_step, 1)
                dve.wait_ge(row_step, 10 * i + 9)
                dve.tensor_scalar(onehot[:, :, :], weight_a[:, :, :], 0.0, None, ALU.is_gt).then_inc(onehot_ready, 1)
                dve.tensor_scalar(row_first, row_first, -float(P), None, ALU.add)
                dve.tensor_scalar(row_second, row_second, -float(P), None, ALU.add).then_inc(row_step, 1)
                dve.wait_ge(row_step, 10 * i + 10)

            def copy_pack(i):
                dve.wait_ge(pack_done, 2 * i + 2)
                dve.tensor_copy(packT[:, 4:8, :], bank[3][:, :].rearrange("p (c q) -> p c q", c=4)).then_inc(pack_b, 1)

            make_onehot(0)
            then(dve.tensor_tensor(over_end[:, :, :], bank[0][:, 0:NE].unsqueeze(2).to_broadcast([P, NE, MAX_OV]),
                                   tile_ends[:, :, :], ALU.is_gt))
            dve.tensor_reduce(tiles_ov[:, :], over_end[:, :, :], AX.X, ALU.add).then_inc(counts_read, 1)
            dve.wait_ge(counts_read, 1)
            then(dve.tensor_copy(scan_a[:, :], tiles_ov[:, :]))
            src, dst, shift = scan_a, scan_b, 1
            while shift < NE:
                dve.tensor_copy(dst[:, 0:shift], src[:, 0:shift])
                then(dve.tensor_tensor(dst[:, shift:], src[:, shift:], src[:, 0:NE - shift], ALU.add))
                src, dst, shift = dst, src, 2 * shift
            sums = src
            then(dve.tensor_tensor(delta[:, :], sums[:, :], tiles_ov[:, :], ALU.subtract))
            then(dve.tensor_scalar(delta[:, :], delta[:, :], float(ROWS), float(ROWS * (NE - 1)) - FAR, ALU.mult, ALU.add))
            then(dve.tensor_tensor(delta[:, :], delta[:, :], first_row[:, :], ALU.subtract))
            then(dve.tensor_tensor(beyond[:, :, :], beyond[:, :, :], wide_e(delta), ALU.mult))
            for chosen, rows in ((sel_a, row_first), (sel_b, row_second)):
                then(dve.tensor_tensor(cand[:, :, :], chosen[:, :, :], beyond[:, :, :], ALU.mult))
                then(dve.tensor_reduce(best, cand[:, :, :], AX.X, ALU.add))
                then(dve.tensor_tensor(rows, rows, best, ALU.add))
            then(dve.tensor_tensor(ov_cmp[:, :, :], sums[0:1, :].unsqueeze(1).to_broadcast([1, OV_TILES, NE]),
                                   ov_iota[:, :].unsqueeze(2).to_broadcast([1, OV_TILES, NE]), ALU.is_le))
            then(dve.tensor_reduce(ov_id[:, :], ov_cmp[:, :, :], AX.X, ALU.add))
            then(dve.tensor_scalar(ov_id[:, :], ov_id[:, :], float(NE - 1), None, ALU.min))
            then(dve.tensor_copy(ov_expert[:, :], ov_id[:, :]))
            dve.tensor_copy(ov_count[:, :], sums[0:1, NE - 1:NE]).then_inc(routed, 1)

            def expert_pair(i):
                copy_pack(i)
                dve.wait_ge(weights_turned, i + 1)
                dve.tensor_reduce(row_weight, bank[7][:, :], AX.X, ALU.add).then_inc(row_weight_ready, 1)
                dve.tensor_scalar(onehotT[:, :], bank[7][:, :], 0.0, None, ALU.is_gt).then_inc(onehotT_ready, 1)
                make_onehot(i + 1)
                dve.wait_ge(silu_ready, i + 1)
                dve.wait_ge(up_done, i + 1)
                dve.tensor_tensor(act_rows[:, :, :].rearrange("q c p -> q p c"),
                                  silu_g[:, :].rearrange("q (p c) -> q p c", c=FT),
                                  bank[1][:, :].rearrange("q (p c) -> q p c", c=FT), ALU.mult).then_inc(rows_ready, 1)
                dve.wait_ge(row_weight_ready, i + 1)
                for n in range(2):
                    dve.wait_ge(y_hi_ready, 2 * i + n + 1)
                    dve.scalar_tensor_tensor(out=y_lo[:, n * 512:(n + 1) * 512], in0=bank[5 + n][:, :], scalar=row_weight,
                                             in1=y_hi[:, n * 512:(n + 1) * 512].bitcast(F32), op0=ALU.mult,
                                             op1=ALU.subtract).then_inc(y_lo_ready, 1)
                for n in range(2):
                    for t in range(TT):
                        dve.wait_ge(spread_done, 8 * i + TT * n + t + 1)
                        part = h_tok[:, t, n * 512:(n + 1) * 512]
                        dve.tensor_tensor(part, bank[SPREAD_BANKS[n][t]][:, :], part, ALU.add).then_inc(h_added, 1)
                dve.wait_ge(h_added, 8 * i + 8)

            with dve.Fori(0, PAIRS) as i:
                expert_pair(i)
            n_over = dve.value_load(ov_count[0:1, 0:1], min_val=0, max_val=OV_TILES)
            with dve.If(n_over > 0):
                with dve.Fori(PAIRS, PAIRS + OV_PAIRS) as i:
                    expert_pair(i)

            dve.memset(root_work, 0.0).then_inc(h_final, 1)
            for t in range(2, TT):
                for n in range(2):
                    last = dve.bn_stats(ln_stats[:, t * 12 + n * 6:t * 12 + (n + 1) * 6], h_tok[:, t, n * 512:(n + 1) * 512])
            then(last)
            for t in range(2, TT):
                last = dve.bn_aggr(ln_mv[:, 2 * t:2 * t + 2], ln_stats[:, t * 12:(t + 1) * 12])
            then(last)
            mean, var = (ln_mv[:, 4:8].rearrange("p (t s) -> p t s", s=2)[:, :, j] for j in range(2))
            then(dve.tensor_tensor(mean_sq[:, 2:4], mean, mean, ALU.mult))
            then(dve.tensor_tensor(mean_sq[:, 2:4], mean_sq[:, 2:4], var, ALU.add))
            dve.wait_ge(ysq_summed, 2)
            inverse_root(rstd, mean_sq)
            dve.memset(root_work, 0.0).then_inc(y_rstd_ready, 1)
            dve.wait_ge(late_loaded, 16 * 6)
            for t in range(2):
                dve.scalar_tensor_tensor(out=result[:, t, :], in0=h_tok[:, t, :], scalar=rstd[:, t:t + 1],
                                         in1=final_g[:, :], op0=ALU.mult, op1=ALU.mult).then_inc(result_low, 1)


_INS = ["x", "norm_mix_g", "w_in", "gate_bias", "gmlp_ln_g", "gmlp_ln_b", "gmlp_w_s", "gmlp_b_s",
        "attn_sinks", "w_branch_a", "w_branch_b", "w_out", "norm_ffn_g", "w_router_group",
        "b_router_group", "w_router_expert", "b_router_expert", "w_gate", "w_up", "w_down",
        "norm_final_g"]


def kernel(**inputs):
    import concourse.bacc as bacc
    from concourse.bass_utils import run_bass_kernel_spmd

    nc = bacc.Bacc("TRN2", target_bir_lowering=False, num_devices=1, dynamic_dma_scratch_size=4096)
    arrays, args = {}, []
    for name in _INS:
        a = np.ascontiguousarray(inputs[name])
        arrays[name] = a
        args.append(nc.dram_tensor(name, a.shape, mybir.dt.from_np(a.dtype), kind="ExternalInput").ap())
    shape = arrays["x"].shape
    args.append(nc.dram_tensor("out", shape, F32, kind="ExternalOutput").ap())
    build_block(nc, *args)
    got = run_bass_kernel_spmd(nc, [arrays], core_ids=[0])
    return got.results[0]["out"]
```
